# Optimizing a Trainium2 kernel written in Bass

```python
import math
import jax, jax.numpy as jnp
from jax import lax
import numpy as np

D_MODEL = 1024
BATCH = 1
SEQ = 128
DEPTH = 1
DEC_BATCH = 1
DEC_SEQ = 512
PAST_LEN = 128

GRID_W = 64
N_HEADS = 8
N_KV_HEADS = 2
GROUP = N_HEADS // N_KV_HEADS
HEAD_DIM = 64
ATTN_WIDTH = N_HEADS * HEAD_DIM
KV_WIDTH = N_KV_HEADS * HEAD_DIM
WINDOW = 128
BLOCK = 128
ROPE_THETA = 10000.0
AXIS_DIM = HEAD_DIM // 2
AXIS_FREQS = AXIS_DIM // 2
CONV_CH = D_MODEL - ATTN_WIDTH
CONV_K = 31
CONV_PAD = CONV_K // 2
IN_WIDTH = ATTN_WIDTH + 2 * KV_WIDTH + 2 * CONV_CH
MIX_WIDTH = ATTN_WIDTH + CONV_CH
N_KEYS = 128
N_EXPERTS = N_KEYS * N_KEYS
PEER_HEADS = 8
PEER_QDIM = 256
PEER_HALF = PEER_QDIM // 2
PEER_TOPK = 16
PEER_TOKEN_BLOCK = 128
EPS = 1e-6

kernel_name = "hybrid_dit_swa_conformer_peer_step"

def rms_norm(x, g):
    xf = x.astype(jnp.float32)
    y = xf * lax.rsqrt(jnp.mean(xf * xf, axis=-1, keepdims=True) + EPS)
    return (y * g.astype(jnp.float32)).astype(x.dtype)

def layer_norm(x, g, b):
    xf = x.astype(jnp.float32)
    mu = jnp.mean(xf, axis=-1, keepdims=True)
    var = jnp.mean(jnp.square(xf - mu), axis=-1, keepdims=True)
    y = (xf - mu) * lax.rsqrt(var + EPS)
    return (y * g.astype(jnp.float32) + b.astype(jnp.float32)).astype(x.dtype)

def axial_rope_tables(seq_len):
    rows = seq_len // GRID_W
    row = jnp.repeat(jnp.arange(rows, dtype=jnp.float32), GRID_W)
    col = jnp.tile(jnp.arange(GRID_W, dtype=jnp.float32), rows)
    inv = ROPE_THETA ** (-jnp.arange(AXIS_FREQS, dtype=jnp.float32) / AXIS_FREQS)
    ang = jnp.concatenate([row[:, None] * inv, col[:, None] * inv], axis=-1)
    return jnp.cos(ang), jnp.sin(ang)

def apply_axial_rope(x, cos, sin):
    xf = x.astype(jnp.float32)
    c = cos[None, :, None, :]
    s = sin[None, :, None, :]

    def rot(t, cc, ss):
        t1, t2 = t[..., :AXIS_FREQS], t[..., AXIS_FREQS:]
        return jnp.concatenate([t1 * cc - t2 * ss, t2 * cc + t1 * ss], axis=-1)

    out = jnp.concatenate([
        rot(xf[..., :AXIS_DIM], c[..., :AXIS_FREQS], s[..., :AXIS_FREQS]),
        rot(xf[..., AXIS_DIM:], c[..., AXIS_FREQS:], s[..., AXIS_FREQS:])], axis=-1)
    return out.astype(x.dtype)

def modulation(cond, w_ada, b_ada):
    m = jax.nn.silu(cond) @ w_ada + b_ada
    return jnp.split(m, 6, axis=-1)

def project(h, w_in, q_norm, k_norm):
    B, S, _ = h.shape
    z = h @ w_in
    q = z[..., :ATTN_WIDTH].reshape(B, S, N_HEADS, HEAD_DIM)
    k = z[..., ATTN_WIDTH:ATTN_WIDTH + KV_WIDTH].reshape(B, S, N_KV_HEADS, HEAD_DIM)
    v = z[..., ATTN_WIDTH + KV_WIDTH:ATTN_WIDTH + 2 * KV_WIDTH].reshape(B, S, N_KV_HEADS, HEAD_DIM)
    u = z[..., ATTN_WIDTH + 2 * KV_WIDTH:]
    return rms_norm(q, q_norm), rms_norm(k, k_norm), v, u

def context_attention(q, k, v, sink):
    B, C = q.shape[:2]
    scale = 1.0 / math.sqrt(HEAD_DIM)
    qg = q.reshape(B, C, N_KV_HEADS, GROUP, HEAD_DIM)
    s = jnp.einsum('bqkgd,bckd->bkgqc', qg, k).astype(jnp.float32) * scale
    s_sink = jnp.broadcast_to(sink.astype(jnp.float32).reshape(1, N_KV_HEADS, GROUP, 1, 1), (B, N_KV_HEADS, GROUP, C, 1))
    p = jax.nn.softmax(jnp.concatenate([s_sink, s], axis=-1), axis=-1)[..., 1:].astype(v.dtype)
    o = jnp.einsum('bkgqc,bckd->bqkgd', p, v)
    return o.reshape(B, C, ATTN_WIDTH)

def latent_attention(q, k, v, k_ctx, v_ctx, sink):
    B, S = q.shape[:2]
    nb = S // BLOCK
    scale = 1.0 / math.sqrt(HEAD_DIM)
    qb = q.reshape(B, nb, BLOCK, N_KV_HEADS, GROUP, HEAD_DIM)
    pad = ((0, 0), (BLOCK, BLOCK), (0, 0), (0, 0))
    kp = jnp.pad(k, pad).reshape(B, nb + 2, BLOCK, N_KV_HEADS, HEAD_DIM)
    vp = jnp.pad(v, pad).reshape(B, nb + 2, BLOCK, N_KV_HEADS, HEAD_DIM)
    kw = jnp.concatenate([kp[:, :-2], kp[:, 1:-1], kp[:, 2:]], axis=2)
    vw = jnp.concatenate([vp[:, :-2], vp[:, 1:-1], vp[:, 2:]], axis=2)
    s_win = jnp.einsum('bnqkgd,bnjkd->bnkgqj', qb, kw).astype(jnp.float32) * scale
    a = jnp.arange(BLOCK)
    j = jnp.arange(3 * BLOCK)
    rel = j[None, :] - BLOCK - a[:, None]
    kpos = (jnp.arange(nb)[:, None] - 1) * BLOCK + j[None, :]
    valid = (jnp.abs(rel) <= WINDOW)[None] & ((kpos >= 0) & (kpos < S))[:, None, :]
    s_win = jnp.where(valid[None, :, None, None], s_win, -jnp.inf)
    s_ctx = jnp.einsum('bnqkgd,bckd->bnkgqc', qb, k_ctx).astype(jnp.float32) * scale
    s_sink = jnp.broadcast_to(sink.astype(jnp.float32).reshape(1, 1, N_KV_HEADS, GROUP, 1, 1),
                              (B, nb, N_KV_HEADS, GROUP, BLOCK, 1))
    p = jax.nn.softmax(jnp.concatenate([s_sink, s_win, s_ctx], axis=-1), axis=-1)
    p_win = p[..., 1:1 + 3 * BLOCK].astype(v.dtype)
    p_ctx = p[..., 1 + 3 * BLOCK:].astype(v.dtype)
    o = (jnp.einsum('bnkgqj,bnjkd->bnqkgd', p_win, vw)
         + jnp.einsum('bnkgqc,bckd->bnqkgd', p_ctx, v_ctx))
    return o.reshape(B, S, ATTN_WIDTH)

def conformer_conv(u, w_dw, b_dw, ln_g, ln_b, w_pw):
    x = u[..., :CONV_CH] * jax.nn.sigmoid(u[..., CONV_CH:])
    y = lax.conv_general_dilated(x, w_dw[:, None, :].astype(x.dtype), window_strides=(1,),
                                 padding=((CONV_PAD, CONV_PAD),),
                                 dimension_numbers=('NWC', 'WIO', 'NWC'),
                                 feature_group_count=CONV_CH) + b_dw
    y = jax.nn.silu(layer_norm(y, ln_g, ln_b))
    return y @ w_pw

def peer(h, w_q, sub_keys, u_tab, v_tab):
    B, S, D = h.shape
    T = B * S
    hf = h.reshape(T, D)
    q = (hf @ w_q).reshape(T, PEER_HEADS, 2, PEER_HALF)
    s1 = jnp.einsum('thd,hkd->thk', q[:, :, 0], sub_keys[:, 0])
    s2 = jnp.einsum('thd,hkd->thk', q[:, :, 1], sub_keys[:, 1])
    v1, i1 = lax.top_k(s1, PEER_TOPK)
    v2, i2 = lax.top_k(s2, PEER_TOPK)
    cand = (v1[..., :, None] + v2[..., None, :]).reshape(T, PEER_HEADS, PEER_TOPK * PEER_TOPK)
    sc, ci = lax.top_k(cand, PEER_TOPK)
    e = (jnp.take_along_axis(i1, ci // PEER_TOPK, axis=-1) * N_KEYS
         + jnp.take_along_axis(i2, ci % PEER_TOPK, axis=-1))
    g = jax.nn.softmax(sc.astype(jnp.float32), axis=-1).astype(h.dtype)
    nblk = T // PEER_TOKEN_BLOCK
    eb = e.reshape(nblk, PEER_TOKEN_BLOCK, PEER_HEADS * PEER_TOPK)
    gb = g.reshape(nblk, PEER_TOKEN_BLOCK, PEER_HEADS * PEER_TOPK)
    xb = hf.reshape(nblk, PEER_TOKEN_BLOCK, D)

    def block(args):
        xt, et, gt = args
        act = jnp.einsum('td,tkd->tk', xt, u_tab[et])
        return jnp.einsum('tk,tkd->td', jax.nn.gelu(act, approximate=False) * gt, v_tab[et])

    out = lax.map(block, (xb, eb, gb))
    return out.reshape(B, S, D)

def trunk_layer(x, cond, norm1, norm2, w_ada, b_ada, w_in, w_out, q_norm, k_norm, attn_sink,
                conv_dw, conv_dw_b, conv_ln_g, conv_ln_b, conv_pw, peer_wq, peer_keys, peer_u, peer_v,
                ctx_kv=None):
    sh1, sc1, g1, sh2, sc2, g2 = modulation(cond, w_ada, b_ada)
    h = rms_norm(x, norm1) * (1.0 + sc1) + sh1
    q, k, v, u = project(h, w_in, q_norm, k_norm)
    if ctx_kv is None:
        attn = context_attention(q, k, v, attn_sink)
        kv_out = (k, v)
    else:
        cos, sin = axial_rope_tables(x.shape[1])
        q = apply_axial_rope(q, cos, sin)
        k = apply_axial_rope(k, cos, sin)
        attn = latent_attention(q, k, v, ctx_kv[0], ctx_kv[1], attn_sink)
        kv_out = None
    conv = conformer_conv(u, conv_dw, conv_dw_b, conv_ln_g, conv_ln_b, conv_pw)
    x = x + g1 * (jnp.concatenate([attn, conv], axis=-1) @ w_out)
    h2 = rms_norm(x, norm2) * (1.0 + sc2) + sh2
    x = x + g2 * peer(h2, peer_wq, peer_keys, peer_u, peer_v)
    return x, kv_out

def setup_inputs(seed: int = 0) -> dict:
    key = jax.random.key(seed)
    ks = jax.random.split(key, 24)
    f = jnp.float32
    n = lambda k, shape, s: jax.random.normal(k, shape, f) * s
    return {
        "x_prompt": n(ks[0], (BATCH, SEQ, D_MODEL), 1.0),
        "x_sample": n(ks[1], (DEC_BATCH, DEC_SEQ, D_MODEL), 1.0),
        "cache_k": n(ks[2], (DEC_BATCH, DEPTH, PAST_LEN, N_KV_HEADS, HEAD_DIM), 1.0),
        "cache_v": n(ks[3], (DEC_BATCH, DEPTH, PAST_LEN, N_KV_HEADS, HEAD_DIM), 1.0),
        "c": n(ks[4], (DEC_BATCH, D_MODEL), 1.0),
        "c_ctx": n(ks[5], (D_MODEL,), 1.0),
        "norm1": 1.0 + n(ks[6], (DEPTH, D_MODEL), 0.01),
        "norm2": 1.0 + n(ks[7], (DEPTH, D_MODEL), 0.01),
        "w_ada": n(ks[8], (DEPTH, D_MODEL, 6 * D_MODEL), 0.5 * D_MODEL ** -0.5),
        "b_ada": n(ks[9], (DEPTH, 6 * D_MODEL), 0.02),
        "w_in": n(ks[10], (DEPTH, D_MODEL, IN_WIDTH), D_MODEL ** -0.5),
        "w_out": n(ks[11], (DEPTH, MIX_WIDTH, D_MODEL), MIX_WIDTH ** -0.5),
        "q_norm": 1.0 + n(ks[12], (DEPTH, HEAD_DIM), 0.01),
        "k_norm": 1.0 + n(ks[13], (DEPTH, HEAD_DIM), 0.01),
        "attn_sink": n(ks[14], (DEPTH, N_HEADS), 0.5),
        "conv_dw": n(ks[15], (DEPTH, CONV_K, CONV_CH), CONV_K ** -0.5),
        "conv_dw_b": n(ks[16], (DEPTH, CONV_CH), 0.02),
        "conv_ln_g": 1.0 + n(ks[17], (DEPTH, CONV_CH), 0.01),
        "conv_ln_b": n(ks[18], (DEPTH, CONV_CH), 0.02),
        "conv_pw": n(ks[19], (DEPTH, CONV_CH, CONV_CH), CONV_CH ** -0.5),
        "peer_wq": n(ks[20], (DEPTH, D_MODEL, PEER_HEADS * PEER_QDIM), D_MODEL ** -0.5),
        "peer_keys": n(ks[21], (DEPTH, PEER_HEADS, 2, N_KEYS, PEER_HALF), PEER_HALF ** -0.5),
        "peer_u": n(ks[22], (DEPTH, N_EXPERTS, D_MODEL), D_MODEL ** -0.5),
        "peer_v": n(ks[23], (DEPTH, N_EXPERTS, D_MODEL), 1.0),
    }

def reference(x_prompt, x_sample, cache_k, cache_v, c, c_ctx, norm1, norm2, w_ada, b_ada, w_in, w_out,
              q_norm, k_norm, attn_sink, conv_dw, conv_dw_b, conv_ln_g, conv_ln_b, conv_pw,
              peer_wq, peer_keys, peer_u, peer_v):
    cond_ctx = c_ctx.reshape(1, 1, D_MODEL)
    cond_lat = c[:, None, :]
    xp = x_prompt
    xs = x_sample
    new_ks = []
    new_vs = []
    for l in range(DEPTH):
        w = (norm1[l], norm2[l], w_ada[l], b_ada[l], w_in[l], w_out[l], q_norm[l], k_norm[l], attn_sink[l],
             conv_dw[l], conv_dw_b[l], conv_ln_g[l], conv_ln_b[l], conv_pw[l],
             peer_wq[l], peer_keys[l], peer_u[l], peer_v[l])
        xp, (k_c, v_c) = trunk_layer(xp, cond_ctx, *w)
        new_ks.append(k_c)
        new_vs.append(v_c)
        xs, _ = trunk_layer(xs, cond_lat, *w, ctx_kv=(cache_k[:, l], cache_v[:, l]))
    new_k = jnp.stack(new_ks, axis=1)
    new_v = jnp.stack(new_vs, axis=1)
    return (xp, xs, new_k, new_v)


_drawn_inputs = setup_inputs


def setup_inputs(seed=0):
    import zlib

    import numpy as np

    out = dict(_drawn_inputs(seed))
    spreads = {}
    factors = {'cache_k': 3.197,
     'cache_v': 11.356,
     'norm1': 5.718,
     'norm2': 11.131,
     'q_norm': 8.0,
     'k_norm': 5.518,
     'attn_sink': 8.0,
     'conv_dw_b': 4.348,
     'conv_ln_g': 36.58,
     'conv_ln_b': 17.754}
    for name, (base, spread) in spreads.items():
        noise = np.random.default_rng([zlib.crc32(name.encode()), seed]).standard_normal(out[name].shape)
        drawn = base * np.exp(spread * noise) if base else spread * noise
        out[name] = __import__('jax').numpy.asarray(drawn.astype(out[name].dtype))
    for name, factor in factors.items():
        out[name] = (out[name] * factor).astype(out[name].dtype)
    return out
```

```python
from contextlib import ExitStack

import concourse.bass as bass
from concourse import mybir

F32 = mybir.dt.float32
BF16 = mybir.dt.bfloat16
U32 = mybir.dt.uint32
ACT = mybir.ActivationFunctionType
ALU = mybir.AluOpType
AX_X = mybir.AxisListType.X

P = 128
D = 1024
DC = D // P
T_P, T_L = 128, 512
TILES = (T_P + T_L) // P
HEADS, KV, HD = 8, 2, 64
QC = HEADS * HD // P
CC = 4
TAPS, PAD = 31, 15
PH = 8
SB = 2 * PH
TOP = 16
SLOTS = PH * TOP
EPS = 1e-6
SCALE = HD ** -0.5
MASKED = -1e30
RUNS = [(0, 1, 16), (1, 1, 8), (2, 1, 5), (3, 1, 4), (4, 1, 3), (5, 3, 2), (8, 8, 1)]
CAND = sum(n * w for _, n, w in RUNS)

RING = 4
N_ADA1, N_IN, N_G1, N_PW, N_OUT, N_ADA2, N_WQ, N_G2 = 16, 14, 8, 4, 8, 16, 16, 8
S_IN, S_PW, S_OUT, S_WQ = (16, 82), (38, 96), (42, 100), (66, 108)
S_ADA1, S_G1, S_ADA2, S_G2 = 0, 30, 50, 124

V_NORM1, V_NORM2, V_BADA, V_COND, V_QG, V_KG, V_CW, V_CB, V_LG, V_LB, V_SINK = 0, 8, 16, 64, 80, 81, 82, 206, 210, 214, 218
V_END = V_SINK + HEADS
C_ID, C_HEAD, C_ROT, C_MASK, C_IOTA, C_COS, C_SIN, C_END = 0, 128, 256, 384, 1024, 1088, 1600, 2112
M_SH1, M_SC1, M_G1, M_SH2, M_SC2, M_G2 = (8 * i for i in range(6))

GR = 8
GB = 16

EV_ACT, EV_DVE = N_IN + N_PW + N_WQ, N_OUT
STATS = 9
UNITS = (2, 8)
UNIT0 = (0, 2)


def build(nc, x_p, x_l, wblk, vecs, consts, kctx, vctx, keys, table, y_p, y_l, o_k, o_v):
    ctx = ExitStack()
    with ctx:
        def sb(name, shape, dt=F32):
            return ctx.enter_context(nc.sbuf_tensor(name, shape, dt))

        def sem(name):
            return ctx.enter_context(nc.semaphore(name))

        xs = (sb("xp", [P, DC, T_P]), sb("xl", [P, DC, T_L]))
        hbuf = sb("h", [P, DC * T_L])
        ring = sb("ring", [P, RING, DC, P])
        vec = sb("vec", [P, V_END])
        con = sb("con", [P, C_END])
        ones = sb("ones", [P, P])
        mod = sb("mod", [P, 48, 2])
        gain = sb("gain", [P, 2, DC])
        scond = sb("scond", [P, DC, 2])
        rb = sb("rb", [P, T_L])
        kc = sb("kc", [P, P])
        vc = sb("vc", [P, P])
        vtok = sb("vtok", [P, 4, P])
        keyT = sb("keyT", [P, SB, P])
        idxu = sb("idxu", [P, TILES, SLOTS], U32)
        gw = sb("gw", [P, TILES, SLOTS])
        h2tok = sb("h2tok", [P, 2, D])
        acc = sb("acc", [P, 2, 2, D])
        arena = sb("arena", [P, 16384])
        zq = arena[:, 0:2560]
        gl = arena[:, 2560:4736]
        ybuf = arena[:, 4736:6784]
        sm = arena[:, 6784:10880].rearrange("p (b h n) -> p b h n", b=2, h=4)
        pt = arena[:, 10880:14976].rearrange("p (b k h n) -> p b k h n", b=2, k=4, h=4)
        qp = arena[:, 8192:16384]
        rows = arena[:, :].rearrange("p (r n) -> p r n", r=GR)
        mix = sb("mix", [P, DC * T_L])
        rope = ybuf.rearrange("p (b t n) -> p b t n", b=2, t=2)
        scr = mix[:, 0:2048].rearrange("p (b n) -> p b n", b=SB)
        cand = mix[:, 2048:2448].rearrange("p (h n) -> p h n", h=PH)
        cand2 = mix[:, 2448:2848].rearrange("p (h n) -> p h n", h=PH)
        eid = mix[:, 2848:3248].rearrange("p (h n) -> p h n", h=PH)
        hit = mix[:, 0:1600].rearrange("p (b k n) -> p b k n", b=2, k=TOP, n=CAND)
        junk = sb("junk", [P, 4, D], BF16)
        best = sb("best", [P, SB, TOP])
        besti = sb("besti", [P, SB, TOP], U32)
        bestf = sb("bestf", [P, SB, TOP])
        top = sb("top", [P, PH, TOP])
        topi = sb("topi", [P, PH, TOP], U32)
        topf = sb("topf", [P, PH, TOP])
        ex = sb("ex", [P, PH, TOP])
        den = sb("den", [P, PH])
        ef = sb("ef", [P, SLOTS])
        mx, nm, sd, rs, es, rd = (sb(n, [P, 2, 4]) for n in ("mx", "nm", "sd", "rs", "es", "rd"))
        ixr = sb("ixr", [P, 2, GR], U32)
        av, ge, cf = (sb(n, [P, GB]) for n in ("av", "ge", "cf"))

        banks = [ctx.enter_context(nc.psum_tensor(f"bank{i}", [P, 512], F32)) for i in range(8)]
        lin, stat, rotb, scb, tpb, pvb = banks[0:2], banks[2], banks[3], banks[4:6], banks[6], banks[7]

        ld_vec = sem("ld_vec"); ld_con = sem("ld_con"); ones_set = sem("ones_set"); cond_set = sem("cond_set")
        mod_set = sem("mod_set"); gain_set = sem("gain_set"); blk_done = sem("blk_done"); squares = sem("squares")
        sums = sem("sums"); sums_read = sem("sums_read"); inverse = sem("inverse"); root = sem("root")
        scaled = sem("scaled"); h_ready = sem("h_ready"); lin_act = sem("lin_act"); lin_dve = sem("lin_dve")
        znorm = sem("znorm"); rot_done = sem("rot_done"); rot_read = sem("rot_read"); qk_ready = sem("qk_ready")
        glu_ready = sem("glu_ready"); sc_done = sem("sc_done"); sc_read = sem("sc_read"); mx_ready = sem("mx_ready")
        ex_done = sem("ex_done"); p_ready = sem("p_ready"); tp_done = sem("tp_done"); tp_read = sem("tp_read")
        pv_done = sem("pv_done"); attn_ready = sem("attn_ready"); conv_step = sem("conv_step"); centred = sem("centred")
        yscaled = sem("yscaled"); y_ready = sem("y_ready"); sk_done = sem("sk_done"); sk_read = sem("sk_read")
        shifted = sem("shifted"); exped = sem("exped"); picked = sem("picked"); h2_tp = sem("h2_tp")
        h2_tok = sem("h2_tok"); dve_step = sem("dve_step"); topk_step = sem("topk_step"); row_used = sem("row_used")
        ix_copied = sem("ix_copied"); paced = sem("paced"); dots = sem("dots"); gelued = sem("gelued")
        coef = sem("coef"); acc_set = sem("acc_set"); summed = sem("summed"); fin_tp = sem("fin_tp")
        fin_read = sem("fin_read"); stored = sem("stored"); kv_stored = sem("kv_stored")
        ldx = [sem(f"ldx{i}") for i in range(2)]
        ring_in = [sem(f"ring_in{i}") for i in range(RING)]
        row_in = [sem(f"row_in{i}") for i in range(GR)]

        block = ctx.enter_context(nc.Block())

        def V(col, n=1):
            return vec[:, col:col + n]

        ident = con[:, C_ID:C_ID + P]

        class Pass:

            def __init__(self, p):
                self.p = p
                self.n = (T_P, T_L)[p]
                self.tiles = self.n // P
                self.x = xs[p]
                self.cond = 1 - p
                n = self.n
                self.h = hbuf[:, 0:DC * n].rearrange("p (c n) -> p c n", c=DC)
                self.z = zq[:, 0:5 * n].rearrange("p (c n) -> p c n", c=5)
                self.r = mix[:, 0:5 * n].rearrange("p (c n) -> p c n", c=5)
                self.gl = gl[:, 0:CC * (n + 2 * PAD)].rearrange("p (c n) -> p c n", c=CC)
                self.y = ybuf[:, 0:CC * n].rearrange("p (c n) -> p c n", c=CC)
                self.zsq = arena[:, 2560:2560 + 5 * n].rearrange("p (c n) -> p c n", c=5)
                self.a = sm[:, 0].rearrange("p h n -> p (h n)")[:, 0:CC * n].rearrange("p (c n) -> p c n", c=CC)
                self.g = sm[:, 1].rearrange("p h n -> p (h n)")[:, 0:CC * n].rearrange("p (c n) -> p c n", c=CC)
                self.mix = mix[:, 0:DC * n].rearrange("p (c n) -> p c n", c=DC)
                self.q = qp[:, 0:SB * n].rearrange("p (c n) -> p c n", c=SB)
                self.rb = rb[:, 0:n]
                self.tile0 = (0, 1)[p]

            def units(self):
                for u in range(UNITS[self.p]):
                    t, g = divmod(u, 2)
                    if self.p == 0:
                        yield u, t, g, [(0, "z", 0, 1)], 2, 1
                    elif t == 0:
                        yield u, t, g, [(0, "z", 0, 2), (2, "c", 0, 1)], 2, 3
                    elif t == self.tiles - 1:
                        yield u, t, g, [(0, "c", 0, 1), (1, "z", t - 1, 2)], 0, 3
                    else:
                        yield u, t, g, [(0, "z", t - 1, 3), (3, "c", 0, 1)], 1, 4

        passes = (Pass(0), Pass(1))
        unit_list = [list(s.units()) for s in passes]

        @block.sync
        def _(sp):
            def load(seq, blk, n):
                def one(j, i=None):
                    at = seq + j
                    src = wblk[blk + j] if i is None else wblk[bass.ds(i * RING + (blk + j), 1)].rearrange("a p c n -> (a p) c n")
                    sp.wait_ge(blk_done, at - RING + 1 if i is None else i * RING + (at - RING + 1))
                    sp.dma_start(ring[:, at % RING], src).then_inc(ring_in[at % RING], 16)
                whole = n // RING
                with sp.Fori(0, whole) as i:
                    for j in range(RING):
                        one(j, i)
                for j in range(whole * RING, n):
                    one(j)

            sp.dma_start(vec[:], vecs).then_inc(ld_vec, 16)
            for j in range(RING):
                sp.dma_start(ring[:, j], wblk[j]).then_inc(ring_in[j], 16)
            sp.dma_start(xs[0][:], x_p).then_inc(ldx[0], 16)
            for dst, src in ((con, consts), (kc, kctx), (vc, vctx), (keyT, keys)):
                sp.dma_start(dst[:], src).then_inc(ld_con, 16)
            sp.dma_start(xs[1][:], x_l).then_inc(ldx[1], 16)
            load(RING, RING, S_WQ[0] + N_WQ - RING)
            load(S_IN[1], S_IN[0], N_IN)
            load(S_PW[1], S_PW[0], N_PW + N_OUT)
            load(S_WQ[1], S_WQ[0], N_WQ)
            load(S_G2, S_WQ[0] + N_WQ, N_G2)
            for t in range(TILES):
                sp.wait_ge(fin_read, DC * (t + 1))
                dst = y_p if t == 0 else y_l[:, :, (t - 1) * P:t * P]
                src = xs[0][:] if t == 0 else xs[1][:, :, (t - 1) * P:t * P]
                sp.dma_start(dst, src).then_inc(stored, 16)
            sp.wait_ge(stored, 16 * TILES)

        @block.tensor
        def _(pe):
            def weights(seq, i=None):
                n = 16 * (seq // RING + 1)
                pe.wait_ge(ring_in[seq % RING], n if i is None else i * 16 + n)
                return ring[:, seq % RING]

            def ada(seq, n):
                with pe.Fori(0, n // RING) as i:
                    for j in range(RING):
                        w = weights(seq + j, i)
                        for c in range(DC):
                            last = pe.matmul(rotb[:, bass.ds(i * (2 * RING) + 2 * j, 2)], w[:, c, :], scond[:, c, :],
                                             start=(c == 0), stop=(c == DC - 1))
                        last.then_inc(blk_done, 1)

            def partition_sum(s, src, chunks, k, w):
                if k or s.p:
                    pe.wait_ge(sums_read, STATS * s.p + k)
                for c in range(chunks):
                    last = pe.matmul(stat[:, 0:s.n], w, src(c), start=(c == 0), stop=(c == chunks - 1))
                last.then_inc(sums, 1)

            def linear(s, bank, w, src, chunks=DC):
                for c in range(chunks):
                    last = pe.matmul(bank[:, 0:s.n], w[:, c, :], src[:, c, :], start=(c == 0), stop=(c == chunks - 1))
                last.then_inc(blk_done, 1)

            def h2_by_token(src, tile, t):
                for half in range(2):
                    if tile:
                        pe.wait_ge(h2_tok, 2 * tile + half - 1)
                    for c in range(4):
                        last = pe.transpose(lin[half][:, c * P:(c + 1) * P], src[:, 4 * half + c, t * P:(t + 1) * P], ident)
                    last.then_inc(h2_tp, 1)

            pe.wait_ge(ones_set, 1)
            pe.wait_ge(cond_set, 1)
            for s in passes:
                n, p = s.n, s.p
                if p == 0:
                    ada(S_ADA1, N_ADA1)
                    pe.wait_ge(ld_con, 64)
                pe.wait_ge(squares, 3 * p + 1)
                partition_sum(s, lambda c: s.h[:, c, :], DC, 0, ones[:])
                pe.wait_ge(h_ready, 16 * p + DC)
                for b in range(N_IN):
                    if b >= 2 or p:
                        pe.wait_ge(lin_act, EV_ACT * p + max(b - 1, 0))
                    if p and b == 0:
                        pe.wait_ge(h2_tok, 2)
                    w = weights(S_IN[p] + b)
                    if b == 1:
                        for t in range(s.tiles):
                            for c in range(DC):
                                last = pe.matmul(lin[1][:, t * P:(t + 1) * P], s.h[:, c, t * P:(t + 1) * P], w[:, c, :],
                                                 start=(c == 0), stop=(c == DC - 1))
                        last.then_inc(blk_done, 1)
                    else:
                        linear(s, lin[b % 2], w, s.h)
                    if 8 <= b < 13:
                        partition_sum(s, lambda c, b=b: s.zsq[:, b - 8, :], 1, b - 7, con[:, C_HEAD:C_HEAD + P])
                if p == 0:
                    pe.wait_ge(mod_set, 1)
                    ada(S_G1, N_G1)
                else:
                    pe.wait_ge(mod_set, 3)
                    for c in range(5):
                        pe.wait_ge(znorm, 5 * p + c + 1)
                        if c:
                            pe.wait_ge(rot_read, c)
                        pe.matmul(rotb[:, 0:n], con[:, C_ROT:C_ROT + P], s.z[:, c, :], start=True, stop=True).then_inc(rot_done, 1)

                def score(unit):
                    u, t, g, spans, _, _ = unit
                    part = slice(HD * g, HD * g + HD)
                    for c in range(QC):
                        k = 4 * (UNIT0[p] + u) + c
                        if k >= 2:
                            pe.wait_ge(sc_read, k - 1)
                        for at, kind, t0, m in spans:
                            kt = s.z[part, 0, t0 * P:(t0 + m) * P] if kind == "z" else kc[part, :]
                            last = pe.matmul(scb[c % 2][:, at * P:(at + m) * P], s.z[part, 1 + c, t * P:(t + 1) * P], kt, start=True, stop=True)
                        last.then_inc(sc_done, 1)

                def values(unit):
                    u, t, g, spans, _, nk = unit
                    un = UNIT0[p] + u
                    for c in range(QC):
                        k = 4 * un + c
                        pe.wait_ge(p_ready, k + 1)
                        if k:
                            pe.wait_ge(tp_read, k)
                        for b in range(nk):
                            last = pe.transpose(tpb[:, b * P:(b + 1) * P], sm[:, u % 2, c, b * P:(b + 1) * P], ident)
                        last.then_inc(tp_done, 1)
                    pe.wait_ge(tp_read, 4 * un + 4)
                    if un:
                        pe.wait_ge(attn_ready, un)
                    kb = 0
                    for at, kind, t0, m in spans:
                        for j in range(m):
                            v = vtok[:, t0 + j, HD * g:HD * g + HD] if kind == "z" else vc[:, HD * g:HD * g + HD]
                            last = pe.matmul(pvb[HD * g:HD * g + HD, :], v, pt[:, u % 2, at + j].rearrange("p h n -> p (h n)"),
                                             start=(kb == 0), stop=(kb == nk - 1))
                            kb += 1
                    last.then_inc(pv_done, 1)

                units = unit_list[p]
                if p:
                    pe.wait_ge(qk_ready, 5)
                else:
                    pe.wait_ge(znorm, 5)
                score(units[0])
                for u, unit in enumerate(units):
                    if u + 1 < len(units):
                        score(units[u + 1])
                    values(unit)
                pe.wait_ge(conv_step, CC * TAPS * (p + 1))
                partition_sum(s, lambda c: s.y[:, c, :], CC, 6, ones[:])
                pe.wait_ge(squares, 3 * p + 2)
                partition_sum(s, lambda c: s.h[:, c, :], CC, 7, ones[:])
                pe.wait_ge(y_ready, CC * (p + 1))
                for b in range(N_PW):
                    pe.wait_ge(lin_act, EV_ACT * p + N_IN + b - 1)
                    linear(s, lin[b % 2], weights(S_PW[p] + b), s.y, CC)
                pe.wait_ge(lin_act, EV_ACT * p + N_IN + N_PW)
                pe.wait_ge(attn_ready, UNIT0[p] + UNITS[p])
                with pe.Fori(0, N_OUT // RING) as i:
                    for j in range(RING):
                        pe.wait_ge(lin_dve, i * RING + (EV_DVE * p + max(j - 1, 0) + 1))
                        linear(s, lin[j % 2], weights(S_OUT[p] + j, i), s.mix)
                if p == 0:
                    pe.wait_ge(mod_set, 2)
                    ada(S_ADA2, N_ADA2)
                pe.wait_ge(squares, 3 * p + 3)
                partition_sum(s, lambda c: s.h[:, c, :], DC, 8, ones[:])
                pe.wait_ge(h_ready, 16 * p + 2 * DC)
                pe.wait_ge(lin_dve, EV_DVE * (p + 1) + 1)
                with pe.Fori(0, N_WQ // RING) as i:
                    for j in range(RING):
                        pe.wait_ge(lin_act, i * RING + (EV_ACT * p + N_IN + N_PW + max(j - 1, 0)))
                        linear(s, lin[j % 2], weights(S_WQ[p] + j, i), s.h)
                pe.wait_ge(lin_act, EV_ACT * (p + 1))
                if p == 0:
                    h2_by_token(s.h, 0, 0)
                for t in range(s.tiles):
                    if s.tile0 + t:
                        pe.wait_ge(sk_read, s.tile0 + t)
                    for b in range(SB):
                        last = pe.matmul(banks[4 + b // 4][:, (b % 4) * P:(b % 4 + 1) * P], s.q[:, b, t * P:(t + 1) * P], keyT[:, b, :],
                                         start=True, stop=True)
                    last.then_inc(sk_done, 1)
            pe.wait_ge(rot_read, 5)
            ada(S_G2, N_G2)
            pe.wait_ge(mod_set, 4)
            h2_by_token(passes[1].h, 1, 0)
            for tile in range(TILES):
                if 1 <= tile < TILES - 1:
                    h2_by_token(passes[1].h, tile + 1, tile)
                pe.wait_ge(summed, tile + 1)
                for half in range(2):
                    if tile:
                        pe.wait_ge(fin_read, DC * (tile - 1) + 4 * half + 4)
                    for c in range(4):
                        last = pe.transpose(banks[2 + half][:, c * P:(c + 1) * P], acc[:, tile % 2, 0, (4 * half + c) * P:(4 * half + c + 1) * P], ident)
                    last.then_inc(fin_tp, 1)

        @block.scalar
        def _(act):
            def sqrt_scale(s, k, r):
                act.wait_ge(inverse, 4 * s.p + k)
                act.activation(r, r, ACT.Sqrt).then_inc(root, 1)

            def add_shift(s, half, col):
                for c in range(DC):
                    act.wait_ge(scaled, 16 * s.p + DC * half + c + 1)
                    act.activation(s.h[:, c, :], s.h[:, c, :], ACT.Identity, bias=mod[:, col + c, s.cond:s.cond + 1]).then_inc(h_ready, 1)

            def h2_evac(tile):
                for half in range(2):
                    act.wait_ge(h2_tp, 2 * tile + half + 1)
                    act.copy(h2tok[:, tile % 2, 512 * half:512 * (half + 1)], lin[half][:]).then_inc(h2_tok, 1)

            act.wait_ge(ld_vec, 16)
            act.activation(scond[:].rearrange("p c k -> p (c k)"), V(V_COND, 2 * DC), ACT.Silu).then_inc(cond_set, 1)
            for s in passes:
                n, p = s.n, s.p
                act.wait_ge(ldx[p], 16)
                if p:
                    act.wait_ge(h2_tp, 2)
                    act.wait_ge(blk_done, S_WQ[0] + N_WQ)
                act.activation(s.h, s.x[:], ACT.Square).then_inc(squares, 1)
                sqrt_scale(s, 1, s.rb)
                act.wait_ge(mod_set, 1)
                add_shift(s, 0, M_SH1)
                if p:
                    act.wait_ge(kv_stored, 32)
                for b in range(N_IN):
                    act.wait_ge(blk_done, S_IN[p] + b + 1)
                    bank = lin[b % 2][:, 0:n]
                    if b == 1:
                        act.copy(vtok[:, 0:s.tiles].rearrange("p t n -> p (t n)"), bank).then_inc(lin_act, 1)
                    elif b < 6:
                        c = max(b - 1, 0)
                        act.copy(s.z[:, c, :], bank)
                        act.activation(s.zsq[:, c, :], bank, ACT.Square).then_inc(lin_act, 1)
                    elif b % 2 == 0:
                        act.copy(s.a[:, (b - 6) // 2, :], bank).then_inc(lin_act, 1)
                    else:
                        act.activation(s.g[:, (b - 6) // 2, :], bank, ACT.Sigmoid).then_inc(lin_act, 1)
                sqrt_scale(s, 2, s.r)
                if p == 0:
                    act.wait_ge(znorm, 1)
                    act.dma_start(o_k, s.z[:, 0, :]).then_inc(kv_stored, 16)
                    act.wait_ge(lin_act, 2)
                    act.dma_start(o_v, vtok[:, 0, :]).then_inc(kv_stored, 16)
                units = unit_list[p]

                def exps(unit):
                    u, _, _, _, _, nk = unit
                    act.wait_ge(mx_ready, UNIT0[p] + u + 1)
                    for c in range(QC):
                        act.activation(sm[:, u % 2, c, 0:nk * P], sm[:, u % 2, c, 0:nk * P], ACT.Exp, bias=nm[:, u % 2, c:c + 1],
                                       accum_out=rs[:, u % 2, c:c + 1])
                    act.activation(es[:, u % 2, :], sd[:, u % 2, :], ACT.Exp).then_inc(ex_done, 1)

                exps(units[0])
                for u, (_, t, g, _, _, nk) in enumerate(units):
                    un = UNIT0[p] + u
                    if u + 1 < len(units):
                        exps(units[u + 1])
                    if un >= 2:
                        act.wait_ge(pv_done, un - 1)
                    for c in range(QC):
                        act.wait_ge(tp_done, 4 * un + c + 1)
                        act.copy(pt[:, u % 2, 0:nk, c, :], tpb[:, 0:nk * P].rearrange("p (k n) -> p k n", k=nk)).then_inc(tp_read, 1)
                    act.wait_ge(pv_done, un + 1)
                    act.copy(s.mix[HD * g:HD * g + HD, 0:QC, t * P:(t + 1) * P],
                             pvb[HD * g:HD * g + HD, :].rearrange("p (h n) -> p h n", h=QC)).then_inc(attn_ready, 1)
                act.wait_ge(centred, CC * (p + 1))
                act.activation(s.h[:, 0:CC, :], s.y, ACT.Square).then_inc(squares, 1)
                sqrt_scale(s, 3, s.rb)
                for c in range(CC):
                    act.wait_ge(yscaled, CC * p + c + 1)
                    act.activation(s.y[:, c, :], s.y[:, c, :], ACT.Silu, bias=V(V_LB + c), scale=V(V_LG + c)).then_inc(y_ready, 1)
                for b in range(N_PW):
                    act.wait_ge(blk_done, S_PW[p] + b + 1)
                    act.copy(s.mix[:, QC + b, :], lin[b % 2][:, 0:n]).then_inc(lin_act, 1)
                act.wait_ge(lin_dve, EV_DVE * (p + 1) + 1)
                act.activation(s.h, s.x[:], ACT.Square).then_inc(squares, 1)
                sqrt_scale(s, 4, s.rb)
                add_shift(s, 1, M_SH2)
                with act.Fori(0, N_WQ // RING) as i:
                    for j in range(RING):
                        act.wait_ge(blk_done, i * RING + (S_WQ[p] + j + 1))
                        act.copy(s.q[:, bass.ds(i * RING + j, 1), :].rearrange("p a n -> p (a n)"), lin[j % 2][:, 0:n]).then_inc(lin_act, 1)
                if p == 0:
                    h2_evac(0)
                for t in range(s.tiles):
                    act.wait_ge(shifted, s.tile0 + t + 1)
                    act.activation(ex[:], ex[:], ACT.Exp).then_inc(exped, 1)
            h2_evac(1)
            for tile in range(TILES):
                if 1 <= tile < TILES - 1:
                    act.wait_ge(summed, tile)
                    h2_evac(tile + 1)
                with act.Fori(0, SLOTS // GB) as i:
                    it = i + tile * (SLOTS // GB)
                    for q in range(GB // 2):
                        act.wait_ge(dots, it * (GB // 2) + (q + 2))
                        act.activation(ge[:, 2 * q:2 * q + 2], av[:, 2 * q:2 * q + 2], ACT.Gelu).then_inc(gelued, 1)
                        act.wait_ge(gelued, it * (GB // 2) + (q + 1))
                        for e in range(2):
                            last = act.activation(cf[:, 2 * q + e:2 * q + e + 1], gw[:, tile, bass.ds(i * GB + (2 * q + e), 1)], ACT.Copy,
                                                  scale=ge[:, 2 * q + e:2 * q + e + 1])
                        last.then_inc(coef, 1)

        @block.vector
        def _(v):
            steps = [0]

            def step(ins):
                steps[0] += 1
                return ins.then_inc(dve_step, 1)

            def settle():
                v.wait_ge(dve_step, steps[0])

            def read_mod(k, seq, n, col):
                v.wait_ge(blk_done, seq + n)
                bias = V(V_BADA + col, n).unsqueeze(2).broadcast_to([P, n, 2])
                v.tensor_tensor(mod[:, col:col + n, :], rotb[:, 0:2 * n].rearrange("p (c k) -> p c k", k=2), bias, ALU.add).then_inc(mod_set, 1)
                v.wait_ge(mod_set, k)

            def norm_gain(s, half, scale_col, norm_col):
                step(v.scalar_tensor_tensor(out=gain[:, half, :], in0=mod[:, scale_col:scale_col + DC, s.cond], scalar=1.0,
                                            in1=V(norm_col, DC), op0=ALU.add, op1=ALU.mult))
                settle()

            def inverse_mean(s, k, r, width, last=True):
                v.wait_ge(sums, STATS * s.p + k + 1)
                v.tensor_scalar(r, stat[:, 0:s.n], 1.0 / width, EPS, ALU.mult, ALU.add).then_inc(sums_read, 1)
                v.wait_ge(sums_read, STATS * s.p + k + 1)
                ins = v.reciprocal(r, r)
                if last:
                    ins.then_inc(inverse, 1)

            def rms_scale(s, half, k, sum_k):
                inverse_mean(s, sum_k, s.rb, D)
                v.wait_ge(root, 4 * s.p + k)
                for c in range(DC):
                    v.scalar_tensor_tensor(out=s.h[:, c, :], in0=s.x[:, c, :], scalar=gain[:, half, c:c + 1], in1=s.rb,
                                           op0=ALU.mult, op1=ALU.mult).then_inc(scaled, 1)

            def taps(s, pair, k0, k1):
                base = CC * TAPS * s.p + 2 * TAPS * pair
                for k in range(k0, k1):
                    for e in range(2):
                        c = 2 * pair + e
                        src = s.gl[:, c, k:k + s.n]
                        w = V(V_CW + TAPS * c + k)
                        if k == 0:
                            ins = v.tensor_scalar(s.y[:, c, :], src, w, V(V_CB + c), ALU.mult, ALU.add)
                        else:
                            v.wait_ge(conv_step, base + 2 * k + e - 1)
                            ins = v.scalar_tensor_tensor(out=s.y[:, c, :], in0=src, scalar=w, in1=s.y[:, c, :], op0=ALU.mult, op1=ALU.add)
                        ins.then_inc(conv_step, 1)

            KT = [None]

            def topk(tile, t0, n):
                def body(i):
                    k = [0]
                    b4 = best[:].rearrange("p (h s) k -> p h s k", s=2)
                    f4 = bestf[:].rearrange("p (h s) k -> p h s k", s=2)

                    def tk(ins):
                        k[0] += 1
                        return ins.then_inc(topk_step, 1)

                    def own():
                        v.wait_ge(topk_step, k[0] if KT[0] is None else (i * KT[0] if i is not None else 0) + (KT[0] * t0 + k[0]))
                        v.sem_inc(paced, 1)

                    def tile_wait(sem_):
                        v.wait_ge(sem_, t0 + 1 if i is None else i + (t0 + 1))
                        v.sem_inc(paced, 1)

                    def sc(b):
                        return banks[4 + b // 4][:, (b % 4) * P:(b % 4 + 1) * P]

                    tile_wait(sk_done)
                    for b in range(SB):
                        tk(v.max(best[:, b, 0:8], sc(b)))
                    own()
                    for b in range(SB):
                        tk(v.max_index(besti[:, b, 0:8], best[:, b, 0:8], sc(b)))
                        ins = tk(v.match_replace(scr[:, b, :], best[:, b, 0:8], sc(b), -3e38))
                    own()
                    v.sem_inc(sk_read, 1)
                    for b in range(SB):
                        tk(v.max(best[:, b, 8:16], scr[:, b, :]))
                    own()
                    for b in range(SB):
                        tk(v.max_index(besti[:, b, 8:16], best[:, b, 8:16], scr[:, b, :]))
                    own()
                    tk(v.tensor_copy(bestf[:], besti[:]))
                    own()
                    tk(v.tensor_scalar(f4[:, :, 0, :], f4[:, :, 0, :], float(P), None, ALU.mult))
                    own()
                    at = 0
                    for i0, rows_, w in RUNS:
                        shape = [P, PH, rows_, w]
                        for dst, src in ((cand, b4), (eid, f4)):
                            tk(v.tensor_tensor(dst[:, :, at:at + rows_ * w].rearrange("p h (r w) -> p h r w", r=rows_),
                                               src[:, :, 0, i0:i0 + rows_].unsqueeze(3).broadcast_to(shape),
                                               src[:, :, 1, 0:w].unsqueeze(2).broadcast_to(shape), ALU.add))
                        at += rows_ * w
                    own()
                    for h in range(PH):
                        tk(v.max(top[:, h, 0:8], cand[:, h, :]))
                    own()
                    for h in range(PH):
                        tk(v.max_index(topi[:, h, 0:8], top[:, h, 0:8], cand[:, h, :]))
                        tk(v.match_replace(cand2[:, h, :], top[:, h, 0:8], cand[:, h, :], -3e38))
                    own()
                    for h in range(PH):
                        tk(v.max(top[:, h, 8:16], cand2[:, h, :]))
                    own()
                    for h in range(PH):
                        tk(v.max_index(topi[:, h, 8:16], top[:, h, 8:16], cand2[:, h, :]))
                    tk(v.tensor_tensor(ex[:], top[:], top[:, :, 0:1].broadcast_to([P, PH, TOP]), ALU.subtract))
                    own()
                    v.sem_inc(shifted, 1)
                    tk(v.tensor_copy(topf[:], topi[:]))
                    own()
                    wide = [P, TOP, CAND]

                    def find(h):
                        tk(v.tensor_tensor(hit[:, h % 2], con[:, C_IOTA:C_IOTA + CAND].unsqueeze(1).broadcast_to(wide),
                                           topf[:, h, :].unsqueeze(2).broadcast_to(wide), ALU.is_equal))

                    find(0)
                    for h in range(PH):
                        own()
                        tk(v.tensor_tensor(hit[:, h % 2], hit[:, h % 2], eid[:, h, :].unsqueeze(1).broadcast_to(wide), ALU.mult))
                        if h + 1 < PH:
                            find(h + 1)
                        own()
                        tk(v.tensor_reduce(ef[:, h * TOP:(h + 1) * TOP], hit[:, h % 2], AX_X, ALU.add))
                    own()
                    dst_i = idxu[:, t0, :] if i is None else idxu[:, bass.ds(i + t0, 1), :].rearrange("p a n -> p (a n)")
                    dst_g = gw[:, t0, :] if i is None else gw[:, bass.ds(i + t0, 1), :].rearrange("p a n -> p (a n)")
                    tk(v.tensor_copy(dst_i, ef[:]))
                    tile_wait(exped)
                    tk(v.tensor_reduce(den[:], ex[:], AX_X, ALU.add))
                    own()
                    tk(v.reciprocal(den[:], den[:]))
                    own()
                    tk(v.tensor_tensor(dst_g.rearrange("p (h k) -> p h k", h=PH), ex[:], den[:].unsqueeze(2).broadcast_to([P, PH, TOP]), ALU.mult))
                    own()
                    v.sem_inc(picked, 1)
                    KT[0] = k[0]

                if n == 1:
                    body(None)
                else:
                    with v.Fori(0, n) as i:
                        body(i)

            for counter in (lin_dve, dots, row_used):
                v.sem_inc(counter, 1)
            v.wait_ge(ld_vec, 16)
            for s in passes:
                n, p = s.n, s.p
                if p == 0:
                    read_mod(1, S_ADA1, N_ADA1, M_SH1)
                norm_gain(s, 0, M_SC1, V_NORM1)
                v.wait_ge(ldx[p], 16)
                rms_scale(s, 0, 1, 0)
                for c in range(5):
                    inverse_mean(s, 1 + c, s.r[:, c, :], HD, last=(c == 4))
                v.wait_ge(root, 4 * p + 2)
                for c in range(5):
                    v.scalar_tensor_tensor(out=s.z[:, c, :], in0=s.z[:, c, :], scalar=V(V_QG if c else V_KG), in1=s.r[:, c, :],
                                           op0=ALU.mult, op1=ALU.mult).then_inc(znorm, 1)
                if p == 0:
                    read_mod(2, S_G1, N_G1, M_G1)
                else:
                    for c in range(5):
                        v.wait_ge(znorm, 5 + c + 1)
                        if c >= 2:
                            v.wait_ge(qk_ready, c - 1)
                        step(v.tensor_tensor(rope[:, c % 2, 0, :], s.z[:, c, :], con[:, C_COS:C_COS + n], ALU.mult))
                        v.wait_ge(rot_done, c + 1)
                        v.tensor_tensor(rope[:, c % 2, 1, :], rotb[:, 0:n], con[:, C_SIN:C_SIN + n], ALU.mult).then_inc(rot_read, 1)
                        settle()
                        v.wait_ge(rot_read, c + 1)
                        v.tensor_tensor(s.z[:, c, :], rope[:, c % 2, 0, :], rope[:, c % 2, 1, :], ALU.add).then_inc(qk_ready, 1)
                v.wait_ge(lin_act, EV_ACT * p + N_IN)
                step(v.memset(s.gl[:, :, 0:PAD], 0.0))
                step(v.memset(s.gl[:, :, PAD + n:], 0.0))
                step(v.tensor_tensor(s.gl[:, :, PAD:PAD + n], s.a, s.g, ALU.mult))
                settle()
                units = unit_list[p]

                def mask_and_max(unit):
                    u, t, g, _, m0, nk = unit
                    un, w = UNIT0[p] + u, nk * P
                    b = u % 2
                    if un >= 2:
                        v.wait_ge(tp_done, 4 * (un - 1))
                        v.wait_ge(ex_done, un - 1)
                    for c in range(QC):
                        v.wait_ge(sc_done, 4 * un + c + 1)
                        v.scalar_tensor_tensor(out=sm[:, b, c, 0:w], in0=scb[c % 2][:, 0:w], scalar=SCALE,
                                               in1=con[:, C_MASK + m0 * P:C_MASK + m0 * P + w], op0=ALU.mult, op1=ALU.add).then_inc(sc_read, 1)
                    v.wait_ge(sc_read, 4 * un + 4)
                    step(v.tensor_reduce(mx[:, b, :], sm[:, b, :, 0:w], AX_X, ALU.max))
                    settle()
                    sink = V(V_SINK + 4 * g, 4)
                    step(v.tensor_tensor(mx[:, b, :], mx[:, b, :], sink, ALU.max))
                    settle()
                    step(v.tensor_scalar(nm[:, b, :], mx[:, b, :], -1.0, None, ALU.mult))
                    v.tensor_tensor(sd[:, b, :], sink, mx[:, b, :], ALU.subtract).then_inc(mx_ready, 1)

                def divide(unit):
                    u, _, _, _, _, nk = unit
                    b = u % 2
                    v.wait_ge(ex_done, UNIT0[p] + u + 1)
                    step(v.tensor_tensor(rd[:, b, :], rs[:, b, :], es[:, b, :], ALU.add))
                    settle()
                    step(v.reciprocal(rd[:, b, :], rd[:, b, :]))
                    settle()
                    for c in range(QC):
                        v.tensor_scalar(sm[:, b, c, 0:nk * P], sm[:, b, c, 0:nk * P], rd[:, b, c:c + 1], None, ALU.mult).then_inc(p_ready, 1)

                mask_and_max(units[0])
                for u, unit in enumerate(units):
                    if u + 1 < len(units):
                        mask_and_max(units[u + 1])
                    if p == 0:
                        taps(s, u, 0, TAPS)
                    else:
                        taps(s, u // 4, 8 * (u % 4), min(TAPS, 8 * (u % 4) + 8))
                    divide(unit)
                v.wait_ge(sums, STATS * p + 7)
                v.tensor_scalar(s.rb, stat[:, 0:n], 1.0 / (CC * P), None, ALU.mult).then_inc(sums_read, 1)
                v.wait_ge(sums_read, STATS * p + 7)
                v.wait_ge(conv_step, CC * TAPS * (p + 1))
                for c in range(CC):
                    v.tensor_tensor(s.y[:, c, :], s.y[:, c, :], s.rb, ALU.subtract).then_inc(centred, 1)
                inverse_mean(s, 7, s.rb, CC * P)
                v.wait_ge(root, 4 * p + 3)
                v.wait_ge(centred, CC * (p + 1))
                for c in range(CC):
                    v.tensor_tensor(s.y[:, c, :], s.y[:, c, :], s.rb, ALU.mult).then_inc(yscaled, 1)
                with v.Fori(0, N_OUT // RING) as i:
                    for j in range(RING):
                        v.wait_ge(blk_done, i * RING + (S_OUT[p] + j + 1))
                        xc = s.x[:, bass.ds(i * RING + j, 1), :].rearrange("p a n -> p (a n)")
                        g1 = mod[:, bass.ds(i * RING + (M_G1 + j), 1), s.cond:s.cond + 1].rearrange("p a n -> p (a n)")
                        v.scalar_tensor_tensor(out=xc, in0=lin[j % 2][:, 0:n], scalar=g1, in1=xc, op0=ALU.mult, op1=ALU.add).then_inc(lin_dve, 1)
                if p == 0:
                    read_mod(3, S_ADA2, N_ADA2, M_SH2)
                norm_gain(s, 1, M_SC2, V_NORM2)
                v.wait_ge(lin_dve, EV_DVE * (p + 1) + 1)
                rms_scale(s, 1, 4, 8)
                topk(s.tile0, s.tile0, s.tiles)
            read_mod(4, S_G2, N_G2, M_G2)

            for tile in range(TILES):
                ab = acc[:, tile % 2]
                if tile >= 2:
                    v.wait_ge(fin_tp, 2 * (tile - 1))
                v.memset(ab, 0.0).then_inc(acc_set, 1)
                v.wait_ge(acc_set, tile + 1)
                v.wait_ge(h2_tok, 2 * (tile + 1))
                with v.Fori(0, SLOTS // GB) as i:
                    it = i + tile * (SLOTS // GB)

                    def dot(q):
                        v.wait_ge(dots, it * (GB // 2) + (max(q - 1, 0) + 1))
                        for e in range(2):
                            sl = 2 * q + e
                            v.wait_ge(row_in[sl % GR], it * (16 * GB // GR) + 16 * (sl // GR + 1))
                            ins = v.scalar_tensor_tensor(out=junk[:, sl % 4, :], in0=rows[:, sl % GR, 0:D], scalar=1.0, in1=h2tok[:, tile % 2, :],
                                                         op0=ALU.mult, op1=ALU.mult, accum_out=av[:, sl:sl + 1])
                        ins.then_inc(dots, 1)

                    def add_rows(q):
                        v.wait_ge(coef, it * (GB // 2) + (q + 1))
                        v.wait_ge(row_used, it * GB + (2 * q + 1))
                        for e in range(2):
                            sl = 2 * q + e
                            v.scalar_tensor_tensor(out=ab[:, e, :], in0=rows[:, sl % GR, D:2 * D], scalar=cf[:, sl:sl + 1], in1=ab[:, e, :],
                                                   op0=ALU.mult, op1=ALU.add).then_inc(row_used, 1)

                    dot(0)
                    for q in range(1, GB // 2):
                        dot(q)
                        add_rows(q - 1)
                    add_rows(GB // 2 - 1)
                v.wait_ge(row_used, SLOTS * (tile + 1) + 1)
                v.tensor_tensor(ab[:, 0, :], ab[:, 0, :], ab[:, 1, :], ALU.add).then_inc(summed, 1)
                s = passes[0 if tile == 0 else 1]
                t = max(tile - 1, 0)
                for c in range(DC):
                    if c % 4 == 0:
                        v.wait_ge(fin_tp, 2 * tile + c // 4 + 1)
                    xc = s.x[:, c, t * P:(t + 1) * P]
                    v.scalar_tensor_tensor(out=xc, in0=banks[2 + c // 4][:, (c % 4) * P:(c % 4 + 1) * P], scalar=mod[:, M_G2 + c, s.cond:s.cond + 1],
                                           in1=xc, op0=ALU.mult, op1=ALU.add).then_inc(fin_read, 1)

        @block.gpsimd
        def _(pool):
            pool.memset(ones[:], 1.0).then_inc(ones_set, 1)
            pool.wait_ge(picked, TILES)

            def gather(tile, i, first):
                base = tile * (SLOTS // GB)
                for half in range(2):
                    k = 2 * base + half + 1
                    at = half * GR if i is None else i * GB + half * GR
                    pool.tensor_copy(ixr[:, half, :], idxu[:, tile, bass.ds(at, GR)]).then_inc(ix_copied, 1)
                    pool.wait_ge(ix_copied, k if i is None else i * 2 + k)
                    pool.sem_inc(paced, 1)
                    for j in range(GR):
                        if not (first and half == 0):
                            used = base * GB + half * GR + j + 2 - GR
                            pool.wait_ge(row_used, used if i is None else i * GB + used)
                            pool.sem_inc(paced, 1)
                        pool.indirect_dma_start(out=rows[:, j, :], out_offset=None, in_=table,
                                                in_offset=bass.IndirectOffsetOnAxis(ap=ixr[:, half, j:j + 1], axis=0)).then_inc(row_in[j], 16)

            gather(0, None, True)
            with pool.Fori(1, SLOTS // GB) as i:
                gather(0, i, False)
            for tile in range(1, TILES):
                with pool.Fori(0, SLOTS // GB) as i:
                    gather(tile, i, False)
    return nc


def constants():
    import numpy as np

    con = np.zeros((P, C_END), np.float32)
    con[:, C_ID:C_ID + P] = np.eye(P)
    con[:, C_HEAD:C_HEAD + P] = np.kron(np.eye(2), np.ones((HD, HD)))
    quarter = HD // 4
    turn = np.zeros((P, P), np.float32)
    for m in range(P):
        if m % (2 * quarter) < quarter:
            turn[m + quarter, m] = -1.0
        else:
            turn[m - quarter, m] = 1.0
    con[:, C_ROT:C_ROT + P] = turn
    q, k = np.arange(P)[:, None], np.arange(P)[None, :]
    con[:, C_MASK + P:C_MASK + 2 * P] = np.where(k >= q, 0.0, MASKED)
    con[:, C_MASK + 3 * P:C_MASK + 4 * P] = np.where(k <= q, 0.0, MASKED)
    con[:, C_IOTA:C_IOTA + CAND] = np.arange(CAND)
    inv = (np.float32(10000.0) ** (-np.arange(quarter, dtype=np.float32) / np.float32(quarter))).astype(np.float32)
    t = np.arange(T_L)
    place = np.stack([t // 64, t % 64]).astype(np.float32)
    d = np.arange(P) % HD
    ang = place[d // (2 * quarter)] * inv[d % quarter][:, None]
    con[:, C_COS:C_COS + T_L] = np.cos(ang)
    con[:, C_SIN:C_SIN + T_L] = np.sin(ang)
    return con


def kernel(x_prompt, x_sample, cache_k, cache_v, c, c_ctx, norm1, norm2, w_ada, b_ada, w_in, w_out, q_norm, k_norm, attn_sink,
           conv_dw, conv_dw_b, conv_ln_g, conv_ln_b, conv_pw, peer_wq, peer_keys, peer_u, peer_v):
    import concourse.bacc as bacc
    import numpy as np
    from concourse.bass_utils import run_bass_kernel_spmd

    def by_feature(x):
        x = np.asarray(x)
        return np.ascontiguousarray(x.reshape(x.shape[0], -1, P).transpose(2, 1, 0))

    def blocks(w):
        w = np.asarray(w)
        w = w.reshape(w.shape[0] // P, P, w.shape[1] // P, P).transpose(2, 1, 0, 3)
        return np.pad(w, ((0, 0), (0, 0), (0, DC - w.shape[2]), (0, 0)))

    a = {k: np.asarray(v) for k, v in dict(ada=w_ada[0], win=w_in[0], wout=w_out[0], pw=conv_pw[0], wq=peer_wq[0]).items()}
    pairs = np.concatenate([np.r_[h * HD:(h + 1) * HD, (h + 4) * HD:(h + 5) * HD] for h in range(4)])
    qw = HEADS * HD
    kvw = KV * HD
    uw = CC * P
    order = [np.arange(qw, qw + 2 * kvw), pairs]
    for j in range(CC):
        order += [np.arange(qw + 2 * kvw + j * P, qw + 2 * kvw + (j + 1) * P), np.arange(qw + 2 * kvw + uw + j * P, qw + 2 * kvw + uw + (j + 1) * P)]
    ada = blocks(a["ada"])
    wblk = np.concatenate([ada[0:16], blocks(a["win"][:, np.concatenate(order)]), ada[16:24], blocks(a["pw"]),
                           blocks(a["wout"][np.r_[pairs, qw:D]]), ada[24:40], blocks(a["wq"]), ada[40:48]])
    vecs = np.zeros((P, V_END), np.float32)

    def put(col, x):
        x = np.asarray(x)
        vecs[:, col:col + x.shape[1]] = x

    put(V_NORM1, np.asarray(norm1[0]).reshape(DC, P).T)
    put(V_NORM2, np.asarray(norm2[0]).reshape(DC, P).T)
    put(V_BADA, np.asarray(b_ada[0]).reshape(48, P).T)
    put(V_COND, np.stack([np.asarray(c[0]).reshape(DC, P).T, np.asarray(c_ctx).reshape(DC, P).T], -1).reshape(P, 2 * DC))
    put(V_QG, np.tile(np.asarray(q_norm[0]), 2)[:, None])
    put(V_KG, np.tile(np.asarray(k_norm[0]), 2)[:, None])
    put(V_CW, np.asarray(conv_dw[0]).reshape(TAPS, CC, P).transpose(2, 1, 0).reshape(P, CC * TAPS))
    put(V_CB, np.asarray(conv_dw_b[0]).reshape(CC, P).T)
    put(V_LG, np.asarray(conv_ln_g[0]).reshape(CC, P).T)
    put(V_LB, np.asarray(conv_ln_b[0]).reshape(CC, P).T)
    put(V_SINK, np.broadcast_to(np.asarray(attn_sink[0])[None], (P, HEADS)))
    ins = {
        "x_p": by_feature(x_prompt[0]),
        "x_l": by_feature(x_sample[0]),
        "wblk": np.ascontiguousarray(wblk),
        "vecs": vecs,
        "consts": constants(),
        "kctx": np.ascontiguousarray(np.asarray(cache_k[0, 0]).reshape(P, kvw).T),
        "vctx": np.ascontiguousarray(np.asarray(cache_v[0, 0]).reshape(P, kvw)),
        "keys": np.ascontiguousarray(np.asarray(peer_keys[0]).reshape(SB, P, P).transpose(2, 0, 1)),
        "table": np.concatenate([np.asarray(peer_u[0]), np.asarray(peer_v[0])], axis=1),
    }
    outs = {"y_p": (P, DC, T_P), "y_l": (P, DC, T_L), "o_k": (P, P), "o_v": (P, P)}
    nc = bacc.Bacc("TRN2", target_bir_lowering=False, num_devices=1)
    args = [nc.dram_tensor(n, x.shape, F32, kind="ExternalInput").ap() for n, x in ins.items()]
    args += [nc.dram_tensor(n, x, F32, kind="ExternalOutput").ap() for n, x in outs.items()]
    build(nc, *args)
    got = run_bass_kernel_spmd(nc, [ins], core_ids=[0]).results[0]

    def by_token(y):
        return np.ascontiguousarray(y.transpose(2, 1, 0).reshape(1, y.shape[2], D))

    new_k = np.ascontiguousarray(got["o_k"].T).reshape(1, 1, P, KV, HD)
    new_v = np.ascontiguousarray(got["o_v"]).reshape(1, 1, P, KV, HD)
    return by_token(got["y_p"]), by_token(got["y_l"]), new_k, new_v
```

```python
from contextlib import ExitStack

import concourse.bass as bass
from concourse import mybir

F32 = mybir.dt.float32
F32R = mybir.dt.float32r
BF16 = mybir.dt.bfloat16
U32 = mybir.dt.uint32
ACT = mybir.ActivationFunctionType
ALU = mybir.AluOpType
AX_X = mybir.AxisListType.X

P = 128
D = 1024
DC = D // P
T_L, T_P = 512, 128
N = T_L + T_P
TILES = N // P
TP = TILES - 1
ORDER = (4, 3, 2, 1, 0)
N_GATHER = 2
N_DENSE = TILES - N_GATHER
ND = N_DENSE * P
HEADS, KV, HD = 8, 2, 64
QC = HEADS * HD // P
QK = QC + 1
CC = 4
TAPS, PAD = 31, 15
NY = T_L + PAD + T_P
YP = T_L + PAD
PH = 8
SB = 2 * PH
TOP = 16
SLOTS = PH * TOP
KEYS = 128
EPS = 1e-6
SCALE = HD ** -0.5
MASKED = -1e30
RUNS = [(0, 1, 16), (1, 1, 8), (2, 1, 5), (3, 1, 4), (4, 1, 3), (5, 3, 2), (8, 8, 1)]
CAND = sum(n * w for _, n, w in RUNS)

RING = 4
N_ADA1, N_IN, N_G1, N_PW, N_OUT, N_ADA2, N_WQ, N_G2 = 16, 14, 8, 4, 8, 16, 16, 8
S_ADA1, S_IN, S_G1, S_PW, S_OUT, S_ADA2, S_WQ, S_G2, S_END = 0, 16, 30, 38, 42, 50, 66, 82, 90

V_NORM1, V_NORM2, V_BADA, V_COND, V_QG, V_KG, V_CW, V_CB, V_LG, V_LB, V_SINK = 0, 8, 16, 64, 80, 81, 82, 206, 210, 214, 218
V_END = V_SINK + HEADS
C_ID, C_ROT, C_MASK, C_IOTA, C_SUM, C_SPREAD, C_COS, C_SIN, C_END = 0, 128, 256, 896, 1024, 1074, 1714, 2226, 2738
M_SH1, M_SC1, M_G1, M_SH2, M_SC2, M_G2 = (8 * i for i in range(6))

GSTEPS = SLOTS // 16
SEARCH_STEPS = 5 * SB + 2 * len(RUNS) + 8 * PH + 8
GR = 4
GB = 16
JB = 8
STEPS = KEYS // JB
TG = 32
NG = ND // TG
QUAD = 4



def attention_units():
    units = []
    for t in (TP, *range(T_L // P)):
        if t == TP:
            spans, m0 = [(0, True, TP, 1)], 2
        elif t == 0:
            spans, m0 = [(0, True, 0, 2), (2, False, 0, 1)], 2
        elif t == T_L // P - 1:
            spans, m0 = [(0, False, 0, 1), (1, True, t - 1, 2)], 0
        else:
            spans, m0 = [(0, True, t - 1, 3), (3, False, 0, 1)], 1
        units += [(t, g, spans, m0, sum(s[3] for s in spans)) for g in range(KV)]
    return units


UNITS = attention_units()

def build(nc, x_in, wblk, vecs, consts, kctx, vctx, keys, table, ublk, y_out, o_k, o_v):
    ctx = ExitStack()
    with ctx:
        def sb(name, shape, dt=F32):
            return ctx.enter_context(nc.sbuf_tensor(name, shape, dt))

        def sem(name):
            return ctx.enter_context(nc.semaphore(name))

        x = sb("x", [P, DC, N])
        vec = sb("vec", [P, V_END])
        con = sb("con", [P, C_END])
        ones = sb("ones", [P, P])
        mod = sb("mod", [P, 48, 2])
        gain = sb("gain", [P, 2, 2, DC])
        scond = sb("scond", [P, DC, 2])
        idxu = sb("idxu", [P, TILES, SLOTS], U32)
        gw = sb("gw", [P, TILES, SLOTS])
        ef = sb("ef", [P, TILES, SLOTS])
        h2tok = sb("h2tok", [P, N_GATHER, D])
        junk = sb("junk", [P, 2, D], BF16)
        best = sb("best", [P, SB, TOP])
        besti = sb("besti", [P, SB, TOP], U32)
        bestf = sb("bestf", [P, SB, TOP])
        top = sb("top", [P, PH, TOP])
        topi = sb("topi", [P, PH, TOP], U32)
        topf = sb("topf", [P, PH, TOP])
        ex = sb("ex", [P, PH, TOP])
        den = sb("den", [P, PH])
        mx, nm, sd, rs, es, rd = (sb(n, [P, 2, 4]) for n in ("mx", "nm", "sd", "rs", "es", "rd"))
        ixr = sb("ixr", [P, 2, 8], U32)
        av, ge, cf = (sb(n, [P, GB]) for n in ("av", "ge", "cf"))
        eT = sb("eT", [P, ND], U32)
        e1T, e2T, gT = (sb(n, [P, ND]) for n in ("e1T", "e2T", "gT"))
        slab = sb("slab", [P, 36864])

        def view(c0, *shape):
            n = 1
            for k in shape:
                n *= k
            flat = slab[:, c0:c0 + n]
            names = "abcd"[:len(shape)]
            if len(shape) == 1:
                return flat
            return flat.rearrange(f"p ({' '.join(names)}) -> p {' '.join(names)}", **dict(zip(names, shape)))

        h = view(0, DC, N)
        ring = view(5120, RING, DC, P)
        keyT = view(9216, SB, P)
        z = view(11264, QK, N)
        GLW = PAD + T_L + PAD + T_P + PAD
        gl = view(14464, CC, GLW)
        y = view(17204, CC, NY)
        sm = view(19824, 2, 4, 512)
        pt = view(23920, 2, 4, 4, P)
        mix = view(28016, DC, N)
        vtok = view(33136, TILES, P)
        rb = view(33776, NY)
        rq = view(34432, N)
        kc = view(35072, P)
        vc = view(35200, P)
        zsq = view(14464, QK, N)
        ga, gg = view(19824, CC, 512), view(23920, CC, 512)
        gap, ggp = view(21872, CC, P), view(25968, CC, P)
        rope = view(17204, 2, 2, 512)
        q = view(11264, SB, N)
        scr = view(28016, SB, P)
        hit = view(28016, 2, TOP, CAND)
        cand, cand2, eid = view(30064, PH, CAND), view(30464, PH, CAND), view(30864, PH, CAND)
        gel, wgt = view(0, 2, ND), view(768, 2, ND)
        accs = (view(9216, 2, D), view(3072, 2, D))
        e1u, e2u = (view(33792 + n, ND).bitcast(U32) for n in (0, ND))
        hot_a, hot_b = view(5120, 4, 4, P), view(7168, 4, 4, P)
        uraw, vraw = view(5120, 2, DC, P), view(7168, 2, D)
        rows = view(11264, GR, 2 * D)
        gbuf = view(19456, 2, KEYS, TG)
        gin = view(33792, 2, NG, QUAD * TG)
        slab_at = nc.lookup_mloc(slab).addr

        def split(name, c0, shape):
            return nc.alloc_sbuf_tensor_at(name, shape, F32R, offset=slab_at + 4 * c0)

        whi, wlo = split("whi", 1536, [P, 2, ND]), split("wlo", 2304, [P, 2, ND])
        uhi, ulo = split("uhi", 19456, [P, 2, DC, P]), split("ulo", 21504, [P, 2, DC, P])
        vhi, vlo = split("vhi", 23552, [P, 2, D]), split("vlo", 25600, [P, 2, D])
        hhi, hlo = split("hhi", 27648, [P, DC, ND]), split("hlo", 30720, [P, DC, ND])
        g_dram = nc.dram_tensor("g_dram", [NG, P, KEYS * TG], F32).ap()

        psum = ctx.enter_context(nc.psum_tensor("psum", [P, 8, 512], F32))

        def bank(b, n=1):
            return psum[:, b:b + n, :].rearrange("p a n -> p (a n)")
        ld_vec = sem("ld_vec"); ld_x = sem("ld_x"); ld_con = sem("ld_con"); ones_set = sem("ones_set"); cond_set = sem("cond_set")
        mod_set = sem("mod_set"); blk_done = sem("blk_done"); squares = sem("squares"); sums = sem("sums"); sums_read = sem("sums_read")
        inverse = sem("inverse"); root = sem("root"); scaled = sem("scaled"); h_ready = sem("h_ready"); lin_act = sem("lin_act")
        lin_dve = sem("lin_dve"); spread = sem("spread"); znorm = sem("znorm"); rot_done = sem("rot_done"); rot_read = sem("rot_read")
        qk_ready = sem("qk_ready"); sc_done = sem("sc_done"); sc_read = sem("sc_read"); mx_ready = sem("mx_ready"); ex_done = sem("ex_done")
        p_ready = sem("p_ready"); tp_done = sem("tp_done"); tp_read = sem("tp_read"); pv_done = sem("pv_done"); attn_ready = sem("attn_ready")
        conv_step = sem("conv_step"); centred = sem("centred"); yscaled = sem("yscaled"); y_ready = sem("y_ready"); sk_done = sem("sk_done")
        sk_read = sem("sk_read"); shifted = sem("shifted"); exped = sem("exped"); picked = sem("picked"); h2_tp = sem("h2_tp")
        h2_tok = sem("h2_tok"); dve_step = sem("dve_step"); topk_step = sem("topk_step"); paced = sem("paced"); paced_pool = sem("paced_pool")
        by_slot = sem("by_slot"); slot_set = sem("slot_set"); halves_set = sem("halves_set"); hot_a_set = sem("hot_a_set"); hot_b_set = sem("hot_b_set")
        g_made = sem("g_made"); g_laid = sem("g_laid"); hsplit = sem("hsplit"); uhi_set = sem("uhi_set"); ulo_set = sem("ulo_set")
        vhi_set = sem("vhi_set"); vlo_set = sem("vlo_set"); act_done = sem("act_done"); gel_set = sem("gel_set"); w_set = sem("w_set")
        whi_set = sem("whi_set"); wlo_set = sem("wlo_set"); out_done = sem("out_done"); row_used = sem("row_used"); ix_copied = sem("ix_copied")
        dots = sem("dots"); gelued = sem("gelued"); coef = sem("coef"); acc_set = sem("acc_set"); summed = sem("summed")
        evacuated = sem("evacuated"); fin_tp = sem("fin_tp"); fin_read = sem("fin_read"); stored = sem("stored"); kv_stored = sem("kv_stored")
        ring_in = [sem(f"ring_in{i}") for i in range(RING)]
        u_in, v_in, g_in, g_out = ([sem(f"{n}{i}") for i in range(2)] for n in ("u_in", "v_in", "g_in", "g_out"))
        row_in = [sem(f"row_in{i}") for i in range(GR)]

        block = ctx.enter_context(nc.Block())

        def V(col, n=1):
            return vec[:, col:col + n]

        ident = con[:, C_ID:C_ID + P]
        lin, stat = (bank(0, 2), bank(2, 2)), bank(4, 2)

        def g_group(b):
            per = P // TG
            return ORDER[N_GATHER + b // per] * per + b % per

        def token_of(b):
            return g_group(b * 4 // TG) * TG + b * 4 % TG

        def final_src(k):
            return accs[k][:, 0, :] if k < N_GATHER else rows[:, k - N_GATHER, 0:D]

        @block.sync
        def _(sp):
            def load(blk, n):
                def one(j, i=None):
                    at = blk + j
                    src = wblk[at] if i is None else wblk[bass.ds(i * RING + at, 1)].rearrange("a p c n -> (a p) c n")
                    sp.wait_ge(blk_done, at - RING + 1 if i is None else i * RING + (at - RING + 1))
                    sp.dma_start(ring[:, at % RING], src).then_inc(ring_in[at % RING], 16)
                whole = n // RING
                with sp.Fori(0, whole) as i:
                    for j in range(RING):
                        one(j, i)
                for j in range(whole * RING, n):
                    one(j)

            sp.dma_start(vec[:], vecs).then_inc(ld_vec, 16)
            for j in range(RING):
                sp.dma_start(ring[:, j], wblk[j]).then_inc(ring_in[j], 16)
            sp.dma_start(x[:], x_in).then_inc(ld_x, 16)
            for dst, src in ((con[:], consts), (kc, kctx), (vc, vctx), (keyT, keys)):
                sp.dma_start(dst, src).then_inc(ld_con, 16)
            load(RING, S_END - RING)

            for b in range(NG):
                sp.wait_ge(g_laid, 8 * (b + 1))
                sp.dma_start(g_dram[g_group(b)], gbuf[:, b % 2].rearrange("p k t -> p (k t)")).then_inc(g_out[b % 2], 16)
            for b in range(2):
                sp.wait_ge(g_out[b], 16 * (NG // 2))
            tv = table.rearrange("(i j) n -> j i n", j=KEYS)
            gv = g_dram.rearrange("g i (q m) -> q i g m", q=KEYS // QUAD)

            def expert_step(i, first):
                for jj in range(JB):
                    b = jj % 2
                    if jj % QUAD == 0:
                        if not first:
                            sp.wait_ge(w_set, i * JB + (jj - QUAD))
                        sp.dma_start(gin[:, jj // QUAD], gv[bass.ds(i * (JB // QUAD) + jj // QUAD, 1)].rearrange("a i g m -> (a i) g m"))\
                            .then_inc(g_in[jj // QUAD], 16)
                    if not (first and jj < 2):
                        sp.wait_ge(ulo_set, i * JB + (jj - 1))
                    sp.dma_start(uraw[:, b], ublk[bass.ds(i * JB + jj, 1)].rearrange("a p c n -> (a p) c n")).then_inc(u_in[b], 16)
                    if not (first and jj < 2):
                        sp.wait_ge(vlo_set, i * JB + (jj - 1))
                    sp.dma_start(vraw[:, b], tv[bass.ds(i * JB + jj, 1), :, D:2 * D].rearrange("a i n -> (a i) n")).then_inc(v_in[b], 16)

            sp.wait_ge(hsplit, 2)
            sp.wait_ge(h2_tok, 2 * N_GATHER)
            expert_step(0, True)
            with sp.Fori(1, STEPS) as i:
                expert_step(i, False)
            for k in range(TILES):
                t = ORDER[k]
                sp.wait_ge(fin_read, DC * (k + 1))
                sp.dma_start(y_out[:, :, t * P:(t + 1) * P], x[:, :, t * P:(t + 1) * P]).then_inc(stored, 16)
            sp.wait_ge(stored, 16 * TILES)

        @block.tensor
        def _(pe):
            def weights(seq, i=None):
                n = 16 * (seq // RING + 1)
                pe.wait_ge(ring_in[seq % RING], n if i is None else i * 16 + n)
                return ring[:, seq % RING]

            def ada(seq, n):
                with pe.Fori(0, n // RING) as i:
                    for j in range(RING):
                        w = weights(seq + j, i)
                        for c in range(DC):
                            last = pe.matmul(psum[:, 7, bass.ds(i * (2 * RING) + 2 * j, 2)], w[:, c, :], scond[:, c, :],
                                             start=(c == 0), stop=(c == DC - 1))
                        last.then_inc(blk_done, 1)

            def both(dst, w, src, l0, p0, start, stop):
                pe.matmul(dst[:, 0:512], w, src[:, l0:l0 + T_L], start=start, stop=stop)
                return pe.matmul(dst[:, 512:N], w, src[:, p0:p0 + T_P], start=start, stop=stop)

            def column_sum(src, chunks, k):
                if k:
                    pe.wait_ge(sums_read, k)
                for c in range(chunks):
                    last = both(stat, ones[:], src[:, c, :], 0, T_L, c == 0, c == chunks - 1)
                last.then_inc(sums, 1)

            def linear(dst, w, src, chunks=DC, p0=T_L):
                for c in range(chunks):
                    last = both(dst, w[:, c, :], src[:, c, :], 0, p0, c == 0, c == chunks - 1)
                last.then_inc(blk_done, 1)

            pe.wait_ge(ones_set, 1)
            pe.wait_ge(cond_set, 1)
            ada(S_ADA1, N_ADA1)
            pe.wait_ge(squares, 1)
            column_sum(h, DC, 0)
            pe.wait_ge(ld_con, 64)
            pe.wait_ge(h_ready, DC)
            for b in range(N_IN):
                if b >= 2:
                    pe.wait_ge(lin_act, b - 1)
                w = weights(S_IN + b)
                if b == 1:
                    for t in range(TILES):
                        for c in range(DC):
                            last = pe.matmul(lin[1][:, t * P:(t + 1) * P], h[:, c, t * P:(t + 1) * P], w[:, c, :],
                                             start=(c == 0), stop=(c == DC - 1))
                    last.then_inc(blk_done, 1)
                else:
                    linear(lin[b % 2], w, h)
                if b == 8:
                    pe.wait_ge(sums_read, 1)
                    for c in range(QK):
                        last = both(stat[0:2 * QK], con[:, C_SUM + 10 * c:C_SUM + 10 * c + 10], zsq[:, c, :], 0, T_L, c == 0, c == QK - 1)
                    last.then_inc(sums, 1)
            pe.wait_ge(mod_set, 1)
            ada(S_G1, N_G1)
            pe.wait_ge(root, 2)
            for c in range(QK):
                pe.wait_ge(sums_read, 2) if c < 1 else pe.wait_ge(znorm, c)
                both(stat, con[0:2 * QK, C_SPREAD + P * c:C_SPREAD + P * (c + 1)], rq[0:2 * QK, :], 0, T_L, True, True).then_inc(spread, 1)
            pe.wait_ge(mod_set, 2)
            for c in range(QK):
                pe.wait_ge(znorm, c + 1)
                if c >= 2:
                    pe.wait_ge(rot_read, c - 1)
                pe.matmul(psum[:, 6 + c % 2, :], con[:, C_ROT:C_ROT + P], z[:, c, 0:T_L], start=True, stop=True).then_inc(rot_done, 1)

            def score(un):
                t, g, spans, _, _ = UNITS[un]
                part = slice(HD * g, HD * g + HD)
                for c in range(QC):
                    k = 4 * un + c
                    if k >= 2:
                        pe.wait_ge(sc_read, k - 1)
                    for at, own, t0, m in spans:
                        kt = z[part, 0, t0 * P:(t0 + m) * P] if own else kc[part, :]
                        last = pe.matmul(psum[:, 6 + c % 2, at * P:(at + m) * P], z[part, 1 + c, t * P:(t + 1) * P], kt, start=True, stop=True)
                    last.then_inc(sc_done, 1)

            def values(un):
                t, g, spans, _, nk = UNITS[un]
                for c in range(QC):
                    k = 4 * un + c
                    pe.wait_ge(p_ready, k + 1)
                    if k >= 2:
                        pe.wait_ge(tp_read, k - 1)
                    for b in range(nk):
                        last = pe.transpose(psum[:, 2 * (k % 2), b * P:(b + 1) * P], sm[:, un % 2, c, b * P:(b + 1) * P], ident)
                    last.then_inc(tp_done, 1)
                pe.wait_ge(tp_read, 4 * un + 4)
                if un >= 2:
                    pe.wait_ge(attn_ready, un - 1)
                kb = 0
                for at, own, t0, m in spans:
                    for j in range(m):
                        v = vtok[:, t0 + j, HD * g:HD * g + HD] if own else vc[:, HD * g:HD * g + HD]
                        last = pe.matmul(psum[HD * g:HD * g + HD, 1 + 2 * (un % 2), :], v, pt[:, un % 2, at + j].rearrange("p h n -> p (h n)"),
                                         start=(kb == 0), stop=(kb == nk - 1))
                        kb += 1
                last.then_inc(pv_done, 1)

            pe.wait_ge(lin_act, N_IN)
            pe.wait_ge(rot_read, QK)
            score(0)
            for un in range(len(UNITS)):
                if un + 1 < len(UNITS):
                    if un + 1 == 2:
                        pe.wait_ge(qk_ready, QK)
                    score(un + 1)
                values(un)
            pe.wait_ge(conv_step, CC * TAPS)
            for k, src in ((2, y), (3, None)):
                pe.wait_ge(znorm, QK)
                if k == 3:
                    pe.wait_ge(sums_read, 3)
                    pe.wait_ge(squares, 2)
                    src = view(0, CC, NY)
                for c in range(CC):
                    pe.matmul(psum[:, 4, :], ones[:], src[:, c, 0:512], start=(c == 0), stop=(c == CC - 1))
                    last = pe.matmul(psum[:, 5, 0:NY - 512], ones[:], src[:, c, 512:NY], start=(c == 0), stop=(c == CC - 1))
                last.then_inc(sums, 1)
            pe.wait_ge(y_ready, CC)
            pe.wait_ge(attn_ready, len(UNITS))
            for b in range(N_PW):
                if b >= 2:
                    pe.wait_ge(lin_act, N_IN + b - 1)
                linear(lin[b % 2], weights(S_PW + b), y, CC, YP)
            pe.wait_ge(lin_act, N_IN + N_PW)
            with pe.Fori(0, N_OUT // RING) as i:
                for j in range(RING):
                    pe.wait_ge(lin_dve, i * RING + (max(j - 1, 0) + 1))
                    linear(lin[j % 2], weights(S_OUT + j, i), mix)
            pe.wait_ge(mod_set, 2)
            ada(S_ADA2, N_ADA2)
            pe.wait_ge(squares, 3)
            column_sum(h, DC, 4)
            pe.wait_ge(h_ready, 2 * DC)
            pe.wait_ge(lin_dve, N_OUT + 1)
            with pe.Fori(0, N_WQ // RING) as i:
                for j in range(RING):
                    pe.wait_ge(lin_act, i * RING + (N_IN + N_PW + max(j - 1, 0)))
                    linear(lin[j % 2], weights(S_WQ + j, i), h)
            pe.wait_ge(lin_act, N_IN + N_PW + N_WQ)
            pe.wait_ge(mod_set, 3)
            ada(S_G2, N_G2)
            pe.wait_ge(mod_set, 4)
            for k, t in enumerate(ORDER):
                if k:
                    pe.wait_ge(sk_read, k)
                for b in range(SB):
                    last = pe.matmul(psum[:, 4 + b // 4, (b % 4) * P:(b % 4 + 1) * P], q[:, b, t * P:(t + 1) * P], keyT[:, b, :],
                                     start=True, stop=True)
                last.then_inc(sk_done, 1)
                if k < N_GATHER:
                    for half in range(2):
                        for c in range(4):
                            last = pe.transpose(psum[:, 2 * k + half, c * P:(c + 1) * P], h[:, 4 * half + c, t * P:(t + 1) * P], ident)
                        last.then_inc(h2_tp, 1)
            pe.wait_ge(h2_tok, 2 * N_GATHER)
            for k in range(N_DENSE):
                pe.wait_ge(picked, N_GATHER + k + 1)
                pe.transpose(psum[:, k, 0:P], ef[:, N_GATHER + k, :], ident)
                pe.transpose(psum[:, k, P:2 * P], gw[:, N_GATHER + k, :], ident).then_inc(by_slot, 1)
            pe.wait_ge(sk_read, TILES)
            for b in range(ND // 4):
                pe.wait_ge(hot_a_set, b + 1)
                pe.wait_ge(hot_b_set, b + 1)
                if b >= 4:
                    pe.wait_ge(g_laid, b - 3)
                for m in range(4):
                    last = pe.matmul(psum[:, 4 + b % 4, m * P:(m + 1) * P], hot_a[:, b % 4, m, :], hot_b[:, b % 4, m, :], start=True, stop=True)
                last.then_inc(g_made, 1)
            pe.wait_ge(g_laid, ND // 4)
            pe.wait_ge(hsplit, 2)

            def activations(i, jj, first):
                b = jj % 2
                pe.wait_ge(uhi_set, i * JB + (jj + 1))
                pe.wait_ge(ulo_set, i * JB + (jj + 1))
                if not (first and jj < 2):
                    pe.wait_ge(gel_set, i * JB + (jj - 1))
                n = 0
                for c in range(DC):
                    for w, m in ((uhi, hhi), (uhi, hlo), (ulo, hhi)):
                        last = pe.matmul(psum[:, b, 0:ND], w[:, b, c, :], m[:, c, :], start=(n == 0), stop=(n == 3 * DC - 1))
                        n += 1
                last.then_inc(act_done, 1)

            def outputs(i, jj, start, stop):
                b = jj % 2
                for s_ in (whi_set, wlo_set, vhi_set, vlo_set):
                    pe.wait_ge(s_, i * JB + (jj - 1))
                for t in range(N_DENSE):
                    for half in range(2):
                        for k, (w, m) in enumerate(((whi, vhi), (whi, vlo), (wlo, vhi))):
                            last = pe.matmul(psum[:, 2 + 2 * t + half, :], w[:, b, t * P:(t + 1) * P], m[:, b, 512 * half:512 * (half + 1)],
                                             start=start and k == 0, stop=stop and k == 2)
                last.then_inc(out_done, 1)

            for jj in range(JB):
                activations(0, jj, True)
                if jj >= 2:
                    outputs(0, jj, jj == 2, False)
            with pe.Fori(1, STEPS) as i:
                for jj in range(JB):
                    activations(i, jj, False)
                    outputs(i, jj, False, False)
            outputs(STEPS, 0, False, False)
            outputs(STEPS, 1, False, True)
            for k in range(TILES):
                if k < N_GATHER:
                    pe.wait_ge(summed, k + 1)
                else:
                    pe.wait_ge(evacuated, k - N_GATHER + 1)
                for half in range(2):
                    if k:
                        pe.wait_ge(fin_read, DC * (k - 1) + 4 * half + 4)
                    for c in range(4):
                        last = pe.transpose(psum[:, half, c * P:(c + 1) * P], final_src(k)[:, (4 * half + c) * P:(4 * half + c + 1) * P], ident)
                    last.then_inc(fin_tp, 1)

        @block.scalar
        def _(act):
            def add_shift(half, col):
                for c in range(DC):
                    act.wait_ge(scaled, DC * half + c + 1)
                    act.activation(h[:, c, 0:T_L], h[:, c, 0:T_L], ACT.Identity, bias=mod[:, col + c, 0:1])
                    act.activation(h[:, c, T_L:N], h[:, c, T_L:N], ACT.Identity, bias=mod[:, col + c, 1:2]).then_inc(h_ready, 1)

            act.wait_ge(ld_vec, 16)
            act.activation(scond[:].rearrange("p c k -> p (c k)"), V(V_COND, 2 * DC), ACT.Silu).then_inc(cond_set, 1)
            act.wait_ge(ld_x, 16)
            act.activation(h, x[:], ACT.Square).then_inc(squares, 1)
            act.wait_ge(inverse, 1)
            act.activation(rb[:, 0:N], rb[:, 0:N], ACT.Sqrt).then_inc(root, 1)
            add_shift(0, M_SH1)
            for b in range(N_IN):
                act.wait_ge(blk_done, S_IN + b + 1)
                src = lin[b % 2][:, 0:N]
                if b == 1:
                    act.copy(vtok.rearrange("p t n -> p (t n)"), src).then_inc(lin_act, 1)
                elif b < 6:
                    c = max(b - 1, 0)
                    act.copy(z[:, c, :], src)
                    act.activation(zsq[:, c, :], src, ACT.Square).then_inc(lin_act, 1)
                else:
                    j = (b - 6) // 2
                    left, right, func = (ga, gap, ACT.Copy) if b % 2 == 0 else (gg, ggp, ACT.Sigmoid)
                    act.activation(left[:, j, :], src[:, 0:T_L], func)
                    act.activation(right[:, j, :], src[:, T_L:N], func).then_inc(lin_act, 1)
            act.wait_ge(inverse, 2)
            act.activation(rq[0:2 * QK, :], rq[0:2 * QK, :], ACT.Sqrt).then_inc(root, 1)

            def exps(un):
                _, _, _, _, nk = UNITS[un]
                act.wait_ge(mx_ready, un + 1)
                b = un % 2
                for c in range(QC):
                    act.activation(sm[:, b, c, 0:nk * P], sm[:, b, c, 0:nk * P], ACT.Exp, bias=nm[:, b, c:c + 1], accum_out=rs[:, b, c:c + 1])
                act.activation(es[:, b, :], sd[:, b, :], ACT.Exp).then_inc(ex_done, 1)

            exps(0)
            for un, (t, g, _, _, nk) in enumerate(UNITS):
                if un + 1 < len(UNITS):
                    exps(un + 1)
                if un >= 2:
                    act.wait_ge(pv_done, un - 1)
                for c in range(QC):
                    k = 4 * un + c
                    act.wait_ge(tp_done, k + 1)
                    act.copy(pt[:, un % 2, 0:nk, c, :], psum[:, 2 * (k % 2), 0:nk * P].rearrange("p (k n) -> p k n", k=nk)).then_inc(tp_read, 1)
                act.wait_ge(pv_done, un + 1)
                act.copy(mix[HD * g:HD * g + HD, 0:QC, t * P:(t + 1) * P],
                         psum[HD * g:HD * g + HD, 1 + 2 * (un % 2), :].rearrange("p (h n) -> p h n", h=QC)).then_inc(attn_ready, 1)
            act.dma_start(o_k, z[:, 0, T_L:N]).then_inc(kv_stored, 16)
            act.dma_start(o_v, vtok[:, TP, :]).then_inc(kv_stored, 16)
            act.wait_ge(centred, CC)
            act.activation(view(0, CC, NY), y, ACT.Square).then_inc(squares, 1)
            act.wait_ge(inverse, 3)
            act.activation(rb, rb, ACT.Sqrt).then_inc(root, 1)
            for c in range(CC):
                act.wait_ge(yscaled, c + 1)
                act.activation(y[:, c, :], y[:, c, :], ACT.Silu, bias=V(V_LB + c), scale=V(V_LG + c)).then_inc(y_ready, 1)
            for b in range(N_PW):
                act.wait_ge(blk_done, S_PW + b + 1)
                act.copy(mix[:, QC + b, :], lin[b % 2][:, 0:N]).then_inc(lin_act, 1)
            act.wait_ge(lin_dve, N_OUT + 1)
            act.activation(h, x[:], ACT.Square).then_inc(squares, 1)
            act.wait_ge(inverse, 4)
            act.activation(rb[:, 0:N], rb[:, 0:N], ACT.Sqrt).then_inc(root, 1)
            add_shift(1, M_SH2)
            act.wait_ge(kv_stored, 32)
            with act.Fori(0, N_WQ // RING) as i:
                for j in range(RING):
                    act.wait_ge(blk_done, i * RING + (S_WQ + j + 1))
                    act.copy(q[:, bass.ds(i * RING + j, 1), :].rearrange("p a n -> p (a n)"), lin[j % 2][:, 0:N]).then_inc(lin_act, 1)
            for k in range(N_GATHER):
                for half in range(2):
                    act.wait_ge(h2_tp, 2 * k + half + 1)
                    act.copy(h2tok[:, k, 512 * half:512 * (half + 1)], psum[:, 2 * k + half, :]).then_inc(h2_tok, 1)
            for k in range(TILES):
                act.wait_ge(shifted, k + 1)
                act.activation(ex[:], ex[:], ACT.Exp).then_inc(exped, 1)
            for k in range(N_DENSE):
                t = ORDER[N_GATHER + k]
                act.wait_ge(by_slot, k + 1)
                act.copy(eT[:, t * P:(t + 1) * P], psum[:, k, 0:P])
                act.copy(gT[:, t * P:(t + 1) * P], psum[:, k, P:2 * P]).then_inc(slot_set, 1)
            act.copy(hhi[:], h[:, :, 0:ND]).then_inc(hsplit, 1)
            for b in range(ND // 4):
                group, m = divmod(b, TG // 4)
                act.wait_ge(g_made, b + 1)
                if m == 0 and group >= 2:
                    act.wait_ge(g_out[group % 2], 16 * (group // 2))
                act.copy(gbuf[:, group % 2, :, 4 * m:4 * m + 4].rearrange("p k t -> p t k"),
                         psum[:, 4 + b % 4, :].rearrange("p (t k) -> p t k", t=4)).then_inc(g_laid, 1)
            for b in range(2):
                act.wait_ge(g_out[b], 16 * (NG // 2))

            def u_lead(i, jj, first):
                b = jj % 2
                act.wait_ge(u_in[b], i * (16 * JB // 2) + 16 * (jj // 2 + 1))
                if not (first and jj < 2):
                    act.wait_ge(act_done, i * JB + (jj - 1))
                act.copy(uhi[:, b], uraw[:, b]).then_inc(uhi_set, 1)

            def v_lead(i, jj, first):
                b = 1 - jj % 2
                act.wait_ge(v_in[b], i * (16 * JB // 2) + 16 * ((jj - 1) // 2 + 1))
                if not (first and jj < 3):
                    act.wait_ge(out_done, i * JB + (jj - 2))
                act.copy(vhi[:, b, :], vraw[:, b, :]).then_inc(vhi_set, 1)

            def w_lead(i, jj):
                act.wait_ge(w_set, i * JB + (jj - 1))
                act.copy(whi[:, jj % 2, :], wgt[:, jj % 2, :]).then_inc(whi_set, 1)

            def gelu(i, jj):
                b = 1 - jj % 2
                act.wait_ge(act_done, i * JB + jj)
                act.activation(gel[:, b, :], psum[:, b, 0:ND], ACT.Gelu).then_inc(gel_set, 1)

            def coefficients(i, k, jj):
                c0 = 2 * ((jj - 1) % JB)
                act.wait_ge(dots, i * (GB // 2) + (jj + 1))
                act.activation(ge[:, c0:c0 + 2], av[:, c0:c0 + 2], ACT.Gelu).then_inc(gelued, 1)
                act.wait_ge(gelued, i * (GB // 2) + jj)
                for e in range(2):
                    g_col = bass.ds(i * GB + (2 * jj - 2 + e - k * SLOTS), 1)
                    last = act.activation(cf[:, c0 + e:c0 + e + 1], gw[:, k, g_col], ACT.Copy, scale=ge[:, c0 + e:c0 + e + 1])
                last.then_inc(coef, 1)

            def expert_step(i, k, before, first=False):
                for jj in range(JB):
                    u_lead(i, jj, first)
                    if not (first and jj < 1):
                        v_lead(i, jj, first)
                    if not (first and jj < 2):
                        w_lead(i, jj)
                    if not (first and jj < 1):
                        coefficients(i, k if jj else before, jj)
                        gelu(i, jj)

            expert_step(0, 0, 0, True)
            for k in range(N_GATHER):
                if k:
                    expert_step(k * GSTEPS, k, k - 1)
                with act.Fori(k * GSTEPS + 1, (k + 1) * GSTEPS) as i:
                    expert_step(i, k, k)
            v_lead(STEPS, 0, False)
            w_lead(STEPS, 0)
            coefficients(STEPS, N_GATHER - 1, 0)
            gelu(STEPS, 0)
            w_lead(STEPS, 1)
            for t in range(N_DENSE):
                k = N_GATHER + t
                act.wait_ge(out_done, KEYS)
                act.wait_ge(summed, N_GATHER)
                act.copy(final_src(k), bank(2 + 2 * ORDER[k], 2)).then_inc(evacuated, 1)

        @block.vector
        def _(v):
            steps = [0]

            def step(ins):
                steps[0] += 1
                return ins.then_inc(dve_step, 1)

            def settle():
                v.wait_ge(dve_step, steps[0])

            def read_mod(k, seq, n, col):
                v.wait_ge(blk_done, seq + n)
                bias = V(V_BADA + col, n).unsqueeze(2).broadcast_to([P, n, 2])
                v.tensor_tensor(mod[:, col:col + n, :], psum[:, 7, 0:2 * n].rearrange("p (c k) -> p c k", k=2), bias, ALU.add).then_inc(mod_set, 1)
                v.wait_ge(mod_set, k)

            def norm_gain(half, scale_col, norm_col):
                for k in range(2):
                    step(v.scalar_tensor_tensor(out=gain[:, half, k, :], in0=mod[:, scale_col:scale_col + DC, k], scalar=1.0,
                                                in1=V(norm_col, DC), op0=ALU.add, op1=ALU.mult))
                settle()

            def inverse_mean(k, r, src, width):
                v.wait_ge(sums, k)
                v.tensor_scalar(r, src, 1.0 / width, EPS, ALU.mult, ALU.add).then_inc(sums_read, 1)
                v.wait_ge(sums_read, k)
                v.reciprocal(r, r).then_inc(inverse, 1)

            def rms_scale(half, sum_k, root_k):
                inverse_mean(sum_k, rb[:, 0:N], stat[:, 0:N], D)
                v.wait_ge(root, root_k)
                for c in range(DC):
                    v.scalar_tensor_tensor(out=h[:, c, 0:T_L], in0=x[:, c, 0:T_L], scalar=gain[:, half, 0, c:c + 1], in1=rb[:, 0:T_L],
                                           op0=ALU.mult, op1=ALU.mult)
                    v.scalar_tensor_tensor(out=h[:, c, T_L:N], in0=x[:, c, T_L:N], scalar=gain[:, half, 1, c:c + 1], in1=rb[:, T_L:N],
                                           op0=ALU.mult, op1=ALU.mult).then_inc(scaled, 1)

            def taps(k0, k1, pair):
                for k in range(k0, k1):
                    for e in range(2):
                        c = 2 * pair + e
                        src = gl[:, c, k:k + NY]
                        w = V(V_CW + TAPS * c + k)
                        if k == 0:
                            ins = v.tensor_scalar(y[:, c, :], src, w, V(V_CB + c), ALU.mult, ALU.add)
                        else:
                            v.wait_ge(conv_step, 2 * TAPS * pair + 2 * k + e - 1)
                            ins = v.scalar_tensor_tensor(out=y[:, c, :], in0=src, scalar=w, in1=y[:, c, :], op0=ALU.mult, op1=ALU.add)
                        ins.then_inc(conv_step, 1)

            for counter in (lin_dve, dots, row_used):
                v.sem_inc(counter, 1)
            v.wait_ge(ld_vec, 16)
            read_mod(1, S_ADA1, N_ADA1, M_SH1)
            norm_gain(0, M_SC1, V_NORM1)
            v.wait_ge(ld_x, 16)
            rms_scale(0, 1, 1)
            inverse_mean(2, rq[0:2 * QK, :], stat[0:2 * QK, 0:N], HD)
            for c in range(QK):
                v.wait_ge(spread, c + 1)
                v.scalar_tensor_tensor(out=z[:, c, :], in0=z[:, c, :], scalar=V(V_QG if c else V_KG), in1=stat[:, 0:N],
                                       op0=ALU.mult, op1=ALU.mult).then_inc(znorm, 1)
            read_mod(2, S_G1, N_G1, M_G1)
            for c in range(QK):
                v.wait_ge(znorm, c + 1)
                if c >= 2:
                    v.wait_ge(qk_ready, c - 1)
                step(v.tensor_tensor(rope[:, c % 2, 0, :], z[:, c, 0:T_L], con[:, C_COS:C_COS + T_L], ALU.mult))
                v.wait_ge(rot_done, c + 1)
                v.tensor_tensor(rope[:, c % 2, 1, :], psum[:, 6 + c % 2, :], con[:, C_SIN:C_SIN + T_L], ALU.mult).then_inc(rot_read, 1)
                settle()
                v.wait_ge(rot_read, c + 1)
                v.tensor_tensor(z[:, c, 0:T_L], rope[:, c % 2, 0, :], rope[:, c % 2, 1, :], ALU.add).then_inc(qk_ready, 1)
            v.wait_ge(lin_act, N_IN)
            step(v.memset(gl[:, :, 0:PAD], 0.0))
            step(v.memset(gl[:, :, PAD + T_L:2 * PAD + T_L], 0.0))
            step(v.memset(gl[:, :, GLW - PAD:], 0.0))
            step(v.tensor_tensor(gl[:, :, PAD:PAD + T_L], ga, gg, ALU.mult))
            step(v.tensor_tensor(gl[:, :, 2 * PAD + T_L:GLW - PAD], gap, ggp, ALU.mult))
            settle()
            v.wait_ge(qk_ready, QK)

            def mask_and_max(un):
                t, g, _, m0, nk = UNITS[un]
                w, b = nk * P, un % 2
                if un >= 2:
                    v.wait_ge(tp_done, 4 * (un - 1))
                    v.wait_ge(ex_done, un - 1)
                for c in range(QC):
                    v.wait_ge(sc_done, 4 * un + c + 1)
                    v.scalar_tensor_tensor(out=sm[:, b, c, 0:w], in0=psum[:, 6 + c % 2, 0:w], scalar=SCALE,
                                           in1=con[:, C_MASK + m0 * P:C_MASK + m0 * P + w], op0=ALU.mult, op1=ALU.add).then_inc(sc_read, 1)
                v.wait_ge(sc_read, 4 * un + 4)
                step(v.tensor_reduce(mx[:, b, :], sm[:, b, :, 0:w], AX_X, ALU.max))
                settle()
                sink = V(V_SINK + 4 * g, 4)
                step(v.tensor_tensor(mx[:, b, :], mx[:, b, :], sink, ALU.max))
                settle()
                step(v.tensor_scalar(nm[:, b, :], mx[:, b, :], -1.0, None, ALU.mult))
                v.tensor_tensor(sd[:, b, :], sink, mx[:, b, :], ALU.subtract).then_inc(mx_ready, 1)

            def divide(un):
                b, nk = un % 2, UNITS[un][4]
                v.wait_ge(ex_done, un + 1)
                step(v.tensor_tensor(rd[:, b, :], rs[:, b, :], es[:, b, :], ALU.add))
                settle()
                step(v.reciprocal(rd[:, b, :], rd[:, b, :]))
                settle()
                for c in range(QC):
                    v.tensor_scalar(sm[:, b, c, 0:nk * P], sm[:, b, c, 0:nk * P], rd[:, b, c:c + 1], None, ALU.mult).then_inc(p_ready, 1)

            mask_and_max(0)
            n_units = len(UNITS)
            for un in range(n_units):
                if un + 1 < n_units:
                    mask_and_max(un + 1)
                pair, part = divmod(un, n_units // 2)
                taps(part * 7 if part else 0, min(TAPS, 7 * (part + 1)), pair)
                divide(un)
            v.wait_ge(sums, 3)
            v.tensor_scalar(rb, stat[:, 0:NY], 1.0 / (CC * P), None, ALU.mult).then_inc(sums_read, 1)
            v.wait_ge(sums_read, 3)
            v.wait_ge(conv_step, CC * TAPS)
            for c in range(CC):
                v.tensor_tensor(y[:, c, :], y[:, c, :], rb, ALU.subtract).then_inc(centred, 1)
            inverse_mean(4, rb, stat[:, 0:NY], CC * P)
            v.wait_ge(root, 3)
            v.wait_ge(centred, CC)
            for c in range(CC):
                v.tensor_tensor(y[:, c, :], y[:, c, :], rb, ALU.mult).then_inc(yscaled, 1)
            with v.Fori(0, N_OUT // RING) as i:
                for j in range(RING):
                    v.wait_ge(blk_done, i * RING + (S_OUT + j + 1))
                    for k, (c0, c1) in enumerate(((0, T_L), (T_L, N))):
                        xc = x[:, bass.ds(i * RING + j, 1), c0:c1].rearrange("p a n -> p (a n)")
                        g1 = mod[:, bass.ds(i * RING + (M_G1 + j), 1), k:k + 1].rearrange("p a n -> p (a n)")
                        last = v.scalar_tensor_tensor(out=xc, in0=lin[j % 2][:, c0:c1], scalar=g1, in1=xc, op0=ALU.mult, op1=ALU.add)
                    last.then_inc(lin_dve, 1)
            read_mod(3, S_ADA2, N_ADA2, M_SH2)
            norm_gain(1, M_SC2, V_NORM2)
            v.wait_ge(lin_dve, N_OUT + 1)
            rms_scale(1, 5, 4)
            read_mod(4, S_G2, N_G2, M_G2)

            def search(i, KT):
                k = [0]
                b4 = best[:].rearrange("p (h s) k -> p h s k", s=2)
                f4 = bestf[:].rearrange("p (h s) k -> p h s k", s=2)

                def tk(ins):
                    k[0] += 1
                    return ins.then_inc(topk_step, 1)

                def hold():
                    v.sem_inc(paced, 1)

                def own():
                    v.wait_ge(topk_step, i * KT + k[0])
                    hold()

                def sc(b):
                    return psum[:, 4 + b // 4, (b % 4) * P:(b % 4 + 1) * P]

                v.wait_ge(sk_done, i + 1)
                hold()
                for b in range(SB):
                    tk(v.max(best[:, b, 0:8], sc(b)))
                own()
                for b in range(SB):
                    tk(v.max_index(besti[:, b, 0:8], best[:, b, 0:8], sc(b)))
                    tk(v.match_replace(scr[:, b, :], best[:, b, 0:8], sc(b), -3e38))
                own()
                v.sem_inc(sk_read, 1)
                for b in range(SB):
                    tk(v.max(best[:, b, 8:16], scr[:, b, :]))
                own()
                for b in range(SB):
                    tk(v.max_index(besti[:, b, 8:16], best[:, b, 8:16], scr[:, b, :]))
                own()
                tk(v.tensor_copy(bestf[:], besti[:]))
                own()
                tk(v.tensor_scalar(f4[:, :, 0, :], f4[:, :, 0, :], float(KEYS), None, ALU.mult))
                own()
                at = 0
                for i0, rows_, w in RUNS:
                    shape = [P, PH, rows_, w]
                    for dst, src in ((cand, b4), (eid, f4)):
                        tk(v.tensor_tensor(dst[:, :, at:at + rows_ * w].rearrange("p h (r w) -> p h r w", r=rows_),
                                           src[:, :, 0, i0:i0 + rows_].unsqueeze(3).broadcast_to(shape),
                                           src[:, :, 1, 0:w].unsqueeze(2).broadcast_to(shape), ALU.add))
                    at += rows_ * w
                own()
                for hd in range(PH):
                    tk(v.max(top[:, hd, 0:8], cand[:, hd, :]))
                own()
                for hd in range(PH):
                    tk(v.max_index(topi[:, hd, 0:8], top[:, hd, 0:8], cand[:, hd, :]))
                    tk(v.match_replace(cand2[:, hd, :], top[:, hd, 0:8], cand[:, hd, :], -3e38))
                own()
                for hd in range(PH):
                    tk(v.max(top[:, hd, 8:16], cand2[:, hd, :]))
                own()
                for hd in range(PH):
                    tk(v.max_index(topi[:, hd, 8:16], top[:, hd, 8:16], cand2[:, hd, :]))
                tk(v.tensor_tensor(ex[:], top[:], top[:, :, 0:1].broadcast_to([P, PH, TOP]), ALU.subtract))
                own()
                v.sem_inc(shifted, 1)
                tk(v.tensor_copy(topf[:], topi[:]))
                own()
                wide = [P, TOP, CAND]

                def find(hd):
                    tk(v.tensor_tensor(hit[:, hd % 2], con[:, C_IOTA:C_IOTA + CAND].unsqueeze(1).broadcast_to(wide),
                                       topf[:, hd, :].unsqueeze(2).broadcast_to(wide), ALU.is_equal))

                dst_e, dst_i, dst_g = (a[:, bass.ds(i, 1), :].rearrange("p a n -> p (a n)") for a in (ef, idxu, gw))
                find(0)
                for hd in range(PH):
                    own()
                    tk(v.tensor_tensor(hit[:, hd % 2], hit[:, hd % 2], eid[:, hd, :].unsqueeze(1).broadcast_to(wide), ALU.mult))
                    if hd + 1 < PH:
                        find(hd + 1)
                    own()
                    tk(v.tensor_reduce(dst_e[:, hd * TOP:(hd + 1) * TOP], hit[:, hd % 2], AX_X, ALU.add))
                own()
                tk(v.tensor_copy(dst_i, dst_e))
                v.wait_ge(exped, i + 1)
                tk(v.tensor_reduce(den[:], ex[:], AX_X, ALU.add))
                own()
                tk(v.reciprocal(den[:], den[:]))
                own()
                tk(v.tensor_tensor(dst_g.rearrange("p (h k) -> p h k", h=PH), ex[:], den[:].unsqueeze(2).broadcast_to([P, PH, TOP]), ALU.mult))
                own()
                v.sem_inc(picked, 1)
                assert k[0] == KT

            with v.Fori(0, TILES) as i:
                search(i, SEARCH_STEPS)

            v.wait_ge(hsplit, 1)
            v.tensor_tensor(hlo[:], h[:, :, 0:ND], hhi[:].bitcast(F32), ALU.subtract).then_inc(hsplit, 1)
            for k in range(N_DENSE):
                t = ORDER[N_GATHER + k]
                part = slice(t * P, (t + 1) * P)
                v.wait_ge(slot_set, k + 1)
                step(v.tensor_scalar(e1u[:, part], eT[:, part], 7, None, ALU.logical_shift_right))
                step(v.tensor_scalar(e2u[:, part], eT[:, part], KEYS - 1, None, ALU.bitwise_and))
                settle()
                step(v.tensor_copy(e1T[:, part], e1u[:, part]))
                step(v.tensor_copy(e2T[:, part], e2u[:, part]))
                settle()
                v.sem_inc(halves_set, 1)
                for b in range(k * P // 4, (k + 1) * P // 4):
                    if b >= 4:
                        v.wait_ge(g_made, b - 3)
                    for m in range(4):
                        col = token_of(b) + m
                        v.tensor_scalar(hot_b[:, b % 4, m, :], con[:, C_IOTA:C_IOTA + KEYS], e2T[:, col:col + 1], gT[:, col:col + 1],
                                        ALU.is_equal, ALU.mult)
                    col = token_of(b) + 2
                    v.tensor_tensor(hot_a[:, b % 4, 2:4, :], con[:, C_IOTA:C_IOTA + KEYS].unsqueeze(1).broadcast_to([P, 2, KEYS]),
                                    e1T[:, col:col + 2].unsqueeze(2).broadcast_to([P, 2, KEYS]), ALU.is_equal).then_inc(hot_b_set, 1)
            for b in range(2):
                v.wait_ge(g_out[b], 16 * (NG // 2))
            for k in range(N_GATHER):
                v.memset(accs[k], 0.0).then_inc(acc_set, 1)
            v.wait_ge(acc_set, N_GATHER)
            v.wait_ge(h2_tok, 2 * N_GATHER)

            def v_rest(i, jj):
                b = 1 - jj % 2
                v.wait_ge(vhi_set, i * JB + jj)
                v.tensor_tensor(vlo[:, b, :], vraw[:, b, :], vhi[:, b, :].bitcast(F32), ALU.subtract).then_inc(vlo_set, 1)

            def w_rest(i, jj):
                b = jj % 2
                v.wait_ge(whi_set, i * JB + (jj - 1))
                v.wait_ge(w_set, i * JB + (jj - 1))
                v.tensor_tensor(wlo[:, b, :], wgt[:, b, :], whi[:, b, :].bitcast(F32), ALU.subtract).then_inc(wlo_set, 1)

            def weigh(i, jj):
                b = 1 - jj % 2
                v.wait_ge(gel_set, i * JB + jj)
                quad, m = divmod(jj - 1, QUAD)
                v.wait_ge(g_in[quad % 2], i * 16 + (0 if quad < 0 else 16))
                v.tensor_tensor(wgt[:, b, :].rearrange("p (g t) -> p g t", t=TG), gel[:, b, :].rearrange("p (g t) -> p g t", t=TG),
                                gin[:, quad % 2, :, m * TG:(m + 1) * TG], ALU.mult).then_inc(w_set, 1)

            def dot(i, k, jj):
                v.wait_ge(dots, i * (GB // 2) + (jj + 1))
                for e in range(2):
                    sl = 2 * jj + e
                    v.wait_ge(row_in[sl % GR], i * (16 * GB // GR) + 16 * (sl // GR + 1))
                    ins = v.scalar_tensor_tensor(out=junk[:, e, :], in0=rows[:, sl % GR, 0:D], scalar=1.0, in1=h2tok[:, k, :],
                                                 op0=ALU.mult, op1=ALU.mult, accum_out=av[:, sl:sl + 1])
                ins.then_inc(dots, 1)

            def add_rows(i, k, jj):
                v.wait_ge(coef, i * (GB // 2) + jj)
                v.wait_ge(row_used, i * GB + (2 * jj - 1))
                for e in range(2):
                    sl = 2 * ((jj - 1) % JB) + e
                    v.scalar_tensor_tensor(out=accs[k][:, e, :], in0=rows[:, sl % GR, D:2 * D], scalar=cf[:, sl:sl + 1], in1=accs[k][:, e, :],
                                           op0=ALU.mult, op1=ALU.add).then_inc(row_used, 1)

            def expert_step(i, k, before, first=False):
                for jj in range(JB):
                    if not (first and jj < 1):
                        v_rest(i, jj)
                    if not (first and jj < 2):
                        w_rest(i, jj)
                    if not (first and jj < 1):
                        add_rows(i, k if jj else before, jj)
                        weigh(i, jj)
                    dot(i, k, jj)

            expert_step(0, 0, 0, True)
            for k in range(N_GATHER):
                if k:
                    expert_step(k * GSTEPS, k, k - 1)
                with v.Fori(k * GSTEPS + 1, (k + 1) * GSTEPS) as i:
                    expert_step(i, k, k)
            v_rest(STEPS, 0)
            w_rest(STEPS, 0)
            add_rows(STEPS, N_GATHER - 1, 0)
            weigh(STEPS, 0)
            w_rest(STEPS, 1)
            v.wait_ge(row_used, N_GATHER * SLOTS + 1)
            for k in range(N_GATHER):
                v.tensor_tensor(accs[k][:, 0, :], accs[k][:, 0, :], accs[k][:, 1, :], ALU.add).then_inc(summed, 1)
            for k in range(TILES):
                t = ORDER[k]
                for c in range(DC):
                    if c % 4 == 0:
                        v.wait_ge(fin_tp, 2 * k + c // 4 + 1)
                    xc = x[:, c, t * P:(t + 1) * P]
                    v.scalar_tensor_tensor(out=xc, in0=psum[:, c // 4, (c % 4) * P:(c % 4 + 1) * P], scalar=mod[:, M_G2 + c, int(t == TP):int(t == TP) + 1],
                                           in1=xc, op0=ALU.mult, op1=ALU.add).then_inc(fin_read, 1)

        @block.gpsimd
        def _(pool):
            pool.memset(ones[:], 1.0).then_inc(ones_set, 1)
            for k in range(N_DENSE):
                pool.wait_ge(halves_set, k + 1)
                for b in range(k * P // 4, (k + 1) * P // 4):
                    if b >= 4:
                        pool.wait_ge(g_made, b - 3)
                    col = token_of(b)
                    for m in range(2):
                        last = pool.tensor_scalar(hot_a[:, b % 4, m, :], con[:, C_IOTA:C_IOTA + KEYS], e1T[:, col + m:col + m + 1], None, ALU.is_equal)
                    last.then_inc(hot_a_set, 1)
            for b in range(2):
                pool.wait_ge(g_out[b], 16 * (NG // 2))

            def fetch_pair(i, k, q_, wait):
                if q_ % 4 == 0:
                    half = q_ // 4
                    pool.tensor_copy(ixr[:, half, :], idxu[:, k, bass.ds(i * GB + (2 * q_ - k * SLOTS), 8)]).then_inc(ix_copied, 1)
                    pool.wait_ge(ix_copied, i * 2 + (half + 1))
                for e in range(2):
                    sl = 2 * q_ + e
                    if wait:
                        pool.wait_ge(row_used, i * GB + (sl + 2 - GR))
                    pool.sem_inc(paced_pool, 1)
                    pool.indirect_dma_start(out=rows[:, sl % GR, :], out_offset=None, in_=table,
                                            in_offset=bass.IndirectOffsetOnAxis(ap=ixr[:, q_ // 4, sl % 8:sl % 8 + 1], axis=0)).then_inc(row_in[sl % GR], 16)

            def expert_step(i, k, first):
                if first:
                    fetch_pair(i, k, 0, False)
                for jj in range(JB):
                    b = jj % 2
                    pool.wait_ge(uhi_set, i * JB + (jj + 1))
                    pool.tensor_tensor(ulo[:, b], uraw[:, b], uhi[:, b].bitcast(F32), ALU.subtract).then_inc(ulo_set, 1)
                    if jj + 1 < JB:
                        fetch_pair(i, k, jj + 1, not (first and jj == 0))
                    else:
                        fetch_next(i, k)

            def fetch_next(i, k):
                pass

            expert_step(0, 0, True)
            for k in range(N_GATHER):
                with pool.Fori(max(1, k * GSTEPS), (k + 1) * GSTEPS) as i:
                    fetch_pair(i, k, 0, True)
                    expert_step(i, k, False)
    return nc


def constants():
    import numpy as np

    con = np.zeros((P, C_END), np.float32)
    con[:, C_ID:C_ID + P] = np.eye(P)
    quarter = HD // 4
    turn = np.zeros((P, P), np.float32)
    for m in range(P):
        if m % (2 * quarter) < quarter:
            turn[m + quarter, m] = -1.0
        else:
            turn[m - quarter, m] = 1.0
    con[:, C_ROT:C_ROT + P] = turn
    q, k = np.arange(P)[:, None], np.arange(P)[None, :]
    con[:, C_MASK + P:C_MASK + 2 * P] = np.where(k >= q, 0.0, MASKED)
    con[:, C_MASK + 3 * P:C_MASK + 4 * P] = np.where(k <= q, 0.0, MASKED)
    con[:, C_IOTA:C_IOTA + KEYS] = np.arange(KEYS)
    for c in range(QK):
        for g in range(2):
            con[HD * g:HD * g + HD, C_SUM + 10 * c + 2 * c + g] = 1.0
            con[2 * c + g, C_SPREAD + P * c + HD * g:C_SPREAD + P * c + HD * g + HD] = 1.0
    inv = (np.float32(10000.0) ** (-np.arange(quarter, dtype=np.float32) / np.float32(quarter))).astype(np.float32)
    t = np.arange(T_L)
    place = np.stack([t // 64, t % 64]).astype(np.float32)
    d = np.arange(P) % HD
    ang = place[d // (2 * quarter)] * inv[d % quarter][:, None]
    con[:, C_COS:C_COS + T_L] = np.cos(ang)
    con[:, C_SIN:C_SIN + T_L] = np.sin(ang)
    return con


def kernel(x_prompt, x_sample, cache_k, cache_v, c, c_ctx, norm1, norm2, w_ada, b_ada, w_in, w_out, q_norm, k_norm, attn_sink,
           conv_dw, conv_dw_b, conv_ln_g, conv_ln_b, conv_pw, peer_wq, peer_keys, peer_u, peer_v):
    import concourse.bacc as bacc
    import numpy as np
    from concourse.bass_utils import run_bass_kernel_spmd

    def by_feature(x):
        x = np.asarray(x)
        return np.ascontiguousarray(x.reshape(x.shape[0], -1, P).transpose(2, 1, 0))

    def blocks(w):
        w = np.asarray(w)
        w = w.reshape(w.shape[0] // P, P, w.shape[1] // P, P).transpose(2, 1, 0, 3)
        return np.pad(w, ((0, 0), (0, 0), (0, DC - w.shape[2]), (0, 0)))

    a = {k: np.asarray(v) for k, v in dict(ada=w_ada[0], win=w_in[0], wout=w_out[0], pw=conv_pw[0], wq=peer_wq[0]).items()}
    pairs = np.concatenate([np.r_[h * HD:(h + 1) * HD, (h + 4) * HD:(h + 5) * HD] for h in range(4)])
    qw = HEADS * HD
    kvw = KV * HD
    uw = CC * P
    order = [np.arange(qw, qw + 2 * kvw), pairs]
    for j in range(CC):
        order += [np.arange(qw + 2 * kvw + j * P, qw + 2 * kvw + (j + 1) * P), np.arange(qw + 2 * kvw + uw + j * P, qw + 2 * kvw + uw + (j + 1) * P)]
    ada = blocks(a["ada"])
    wblk = np.concatenate([ada[0:16], blocks(a["win"][:, np.concatenate(order)]), ada[16:24], blocks(a["pw"]),
                           blocks(a["wout"][np.r_[pairs, qw:D]]), ada[24:40], blocks(a["wq"]), ada[40:48]])
    vecs = np.zeros((P, V_END), np.float32)

    def put(col, x):
        x = np.asarray(x)
        vecs[:, col:col + x.shape[1]] = x

    put(V_NORM1, np.asarray(norm1[0]).reshape(DC, P).T)
    put(V_NORM2, np.asarray(norm2[0]).reshape(DC, P).T)
    put(V_BADA, np.asarray(b_ada[0]).reshape(48, P).T)
    put(V_COND, np.stack([np.asarray(c[0]).reshape(DC, P).T, np.asarray(c_ctx).reshape(DC, P).T], -1).reshape(P, 2 * DC))
    put(V_QG, np.tile(np.asarray(q_norm[0]), 2)[:, None])
    put(V_KG, np.tile(np.asarray(k_norm[0]), 2)[:, None])
    put(V_CW, np.asarray(conv_dw[0]).reshape(TAPS, CC, P).transpose(2, 1, 0).reshape(P, CC * TAPS))
    put(V_CB, np.asarray(conv_dw_b[0]).reshape(CC, P).T)
    put(V_LG, np.asarray(conv_ln_g[0]).reshape(CC, P).T)
    put(V_LB, np.asarray(conv_ln_b[0]).reshape(CC, P).T)
    put(V_SINK, np.broadcast_to(np.asarray(attn_sink[0])[None], (P, HEADS)))
    ins = {
        "x_in": by_feature(np.concatenate([np.asarray(x_sample[0]), np.asarray(x_prompt[0])])),
        "wblk": np.ascontiguousarray(wblk),
        "vecs": vecs,
        "consts": constants(),
        "kctx": np.ascontiguousarray(np.asarray(cache_k[0, 0]).reshape(P, kvw).T),
        "vctx": np.ascontiguousarray(np.asarray(cache_v[0, 0]).reshape(P, kvw)),
        "keys": np.ascontiguousarray(np.asarray(peer_keys[0]).reshape(SB, P, P).transpose(2, 0, 1)),
        "table": np.concatenate([np.asarray(peer_u[0]), np.asarray(peer_v[0])], axis=1),
        "ublk": np.ascontiguousarray(np.asarray(peer_u[0]).reshape(KEYS, KEYS, DC, P).transpose(1, 3, 2, 0)),
    }
    outs = {"y_out": (P, DC, N), "o_k": (P, P), "o_v": (P, P)}
    nc = bacc.Bacc("TRN2", target_bir_lowering=False, num_devices=1)
    args = [nc.dram_tensor(n, x.shape, F32, kind="ExternalInput").ap() for n, x in ins.items()]
    args += [nc.dram_tensor(n, x, F32, kind="ExternalOutput").ap() for n, x in outs.items()]
    build(nc, *args)
    got = run_bass_kernel_spmd(nc, [ins], core_ids=[0]).results[0]

    def by_token(y):
        return np.ascontiguousarray(y.transpose(2, 1, 0).reshape(1, y.shape[2], D))

    new_k = np.ascontiguousarray(got["o_k"].T).reshape(1, 1, P, KV, HD)
    new_v = np.ascontiguousarray(got["o_v"]).reshape(1, 1, P, KV, HD)
    return by_token(got["y_out"][:, :, T_L:]), by_token(got["y_out"][:, :, :T_L]), new_k, new_v
```

```python
from contextlib import ExitStack

import concourse.bass as bass
from concourse import mybir

F32 = mybir.dt.float32
F32R = mybir.dt.float32r
BF16 = mybir.dt.bfloat16
U32 = mybir.dt.uint32
ACT = mybir.ActivationFunctionType
ALU = mybir.AluOpType
AX_X = mybir.AxisListType.X

P = 128
D = 1024
DC = D // P
T_L, T_P = 512, 128
N = T_L + T_P
TILES = N // P
TP = TILES - 1
ORDER = (4, 3, 2, 1, 0)
N_GATHER = 2
N_DENSE = TILES - N_GATHER
ND = N_DENSE * P
HEADS, KV, HD = 8, 2, 64
QC = HEADS * HD // P
QK = QC + 1
CC = 4
TAPS, PAD = 31, 15
NY = T_L + PAD + T_P
YP = T_L + PAD
PH = 8
SB = 2 * PH
TOP = 16
SLOTS = PH * TOP
KEYS = 128
EPS = 1e-6
SCALE = HD ** -0.5
MASKED = -1e30
RUNS = [(0, 1, 16), (1, 1, 8), (2, 1, 5), (3, 1, 4), (4, 1, 3), (5, 3, 2), (8, 8, 1)]
CAND = sum(n * w for _, n, w in RUNS)

RING = 4
N_ADA1, N_IN, N_ADA2, N_PW, N_OUT, N_WQ, N_ADA3 = 16, 14, 24, 4, 8, 16, 8
S_ADA1, S_IN, S_ADA2, S_PW, S_OUT, S_WQ, S_ADA3, S_END = 0, 16, 30, 54, 58, 66, 82, 90
ADA_G = 4
ADA_EARLY = 3
IN_K, IN_V = 2 * CC, 2 * CC + 1

V_NORM1, V_NORM2, V_BADA, V_COND, V_QG, V_KG, V_CW, V_CB, V_LG, V_LB, V_SINK = 0, 8, 16, 64, 80, 81, 82, 206, 210, 214, 218
V_END = V_SINK + HEADS
C_ID, C_ROT, C_MASK, C_IOTA, C_SUM, C_SPREAD, C_COS, C_SIN, C_END = 0, 128, 256, 896, 1024, 1074, 1714, 2226, 2738
M_SH1, M_SC1, M_G1, M_SH2, M_SC2, M_G2 = (8 * i for i in range(6))

GSTEPS = SLOTS // 16
NUMBER_STEPS = 2 + len(RUNS)
HEAD_STEPS = 2 * 5 * TILES + len(RUNS) + 5 * TILES + 2
GR = 4
GB = 16
JB = 8
STEPS = KEYS // JB
TG = 32
NG = ND // TG
QUAD = 4


def attention_units():
    units = []
    for t in (TP, *range(T_L // P)):
        if t == TP:
            spans, m0 = [(0, True, TP, 1)], 2
        elif t == 0:
            spans, m0 = [(0, True, 0, 2), (2, False, 0, 1)], 2
        elif t == T_L // P - 1:
            spans, m0 = [(0, False, 0, 1), (1, True, t - 1, 2)], 0
        else:
            spans, m0 = [(0, True, t - 1, 3), (3, False, 0, 1)], 1
        units += [(t, g, spans, m0, sum(s[3] for s in spans)) for g in range(KV)]
    return units


UNITS = attention_units()


def build(nc, x_in, wblk, vecs, consts, kctx, vctx, keys, table, ublk, y_out, o_k, o_v):
    ctx = ExitStack()
    with ctx:
        def sb(name, shape, dt=F32):
            return ctx.enter_context(nc.sbuf_tensor(name, shape, dt))

        def sem(name):
            return ctx.enter_context(nc.semaphore(name))

        x = sb("x", [P, DC, N])
        vec = sb("vec", [P, V_END])
        con = sb("con", [P, C_END])
        ones = sb("ones", [P, P])
        mod = sb("mod", [P, 48, 2])
        gain = sb("gain", [P, 2, 2, DC])
        scond = sb("scond", [P, DC, 2])
        idxu = sb("idxu", [P, TILES, SLOTS], U32)
        gw = sb("gw", [P, TILES, SLOTS])
        ef = sb("ef", [P, TILES, SLOTS])
        h2tok = sb("h2tok", [P, N_GATHER, D])
        junk = sb("junk", [P, 2, D], BF16)
        bestf = sb("bestf", [P, TILES, 2, TOP])
        top = sb("top", [P, TILES, TOP])
        topi = sb("topi", [P, TILES, TOP], U32)
        topf = sb("topf", [P, TILES, TOP], BF16)
        count = sb("count", [P, CAND], BF16)
        den = sb("den", [P, TILES * PH])
        mx, nm, sd, rs, es, rd = (sb(n, [P, 2, 4]) for n in ("mx", "nm", "sd", "rs", "es", "rd"))
        ixr = sb("ixr", [P, 2, 8], U32)
        av, ge, cf = (sb(n, [P, GB]) for n in ("av", "ge", "cf"))
        eT = sb("eT", [P, ND], U32)
        e1T, e2T, gT = (sb(n, [P, ND]) for n in ("e1T", "e2T", "gT"))
        slab = sb("slab", [P, 36864])

        def view(c0, *shape):
            n = 1
            for k in shape:
                n *= k
            flat = slab[:, c0:c0 + n]
            names = "abcd"[:len(shape)]
            if len(shape) == 1:
                return flat
            return flat.rearrange(f"p ({' '.join(names)}) -> p {' '.join(names)}", **dict(zip(names, shape)))

        h = view(0, DC, N)
        ring = view(5120, RING, DC, P)
        keyT = view(9216, SB, P)
        z = view(11264, QK, N)
        GLW = PAD + T_L + PAD + T_P + PAD
        gl = view(14464, CC, GLW)
        y = view(17204, CC, NY)
        sm = view(19824, 2, 4, 512)
        pt = view(23920, 2, 4, 4, P)
        mix = view(28016, DC, N)
        vtok = view(33136, TILES, P)
        rb = view(33776, NY)
        rq = view(34432, N)
        kc = view(35072, P)
        vc = view(35200, P)
        zsq = view(28016, QK, N)
        ga, gg = view(19824, CC, 512), view(23920, CC, 512)
        gap, ggp = view(21872, CC, P), view(25968, CC, P)
        rope = view(28016, 2, 2, 512)
        modrow = (view(19824, 4, ADA_G * P), view(3072, 4, ADA_G * P), view(9216, 2, ADA_G * P))
        q = view(11264, RING, N)
        best, besti = view(21504, TILES, 2, TOP), view(21664, TILES, 2, TOP).bitcast(U32)
        scr = view(25344, 2, TILES, P)
        hit = view(13824, TILES, TOP, CAND)
        place = view(22784, TILES * TOP * CAND // 2).bitcast(BF16).rearrange("p (t k n) -> p t k n", t=TILES, k=TOP)
        cand, cand2, eid = view(17824, TILES, CAND), view(18080, TILES, CAND), view(18336, TILES, CAND)
        ex = view(18608, TILES, PH, TOP)
        gel, wgt = view(0, 2, ND), view(768, 2, ND)
        accs = (view(9216, 2, D), view(3072, 2, D))
        e1u, e2u = (view(33792 + n, ND).bitcast(U32) for n in (0, ND))
        gnT, away = view(34560, ND), view(34944, 4, KEYS)
        hot_a, hot_b = view(5120, 4, 4, P), view(7168, 4, 4, P)
        uraw, vraw = view(5120, 2, DC, P), view(7168, 2, D)
        rows = view(11264, GR, 2 * D)
        gbuf = view(19456, 2, KEYS, TG)
        gin = view(33792, 2, NG, QUAD * TG)
        slab_at = nc.lookup_mloc(slab).addr

        def split(name, c0, shape):
            return nc.alloc_sbuf_tensor_at(name, shape, F32R, offset=slab_at + 4 * c0)

        whi, wlo = split("whi", 1536, [P, 2, ND]), split("wlo", 2304, [P, 2, ND])
        uhi, ulo = split("uhi", 19456, [P, 2, DC, P]), split("ulo", 21504, [P, 2, DC, P])
        vhi, vlo = split("vhi", 23552, [P, 2, D]), split("vlo", 25600, [P, 2, D])
        hhi, hlo = split("hhi", 27648, [P, DC, ND]), split("hlo", 30720, [P, DC, ND])
        g_dram = nc.dram_tensor("g_dram", [NG, P, KEYS * TG], F32).ap()

        psum = ctx.enter_context(nc.psum_tensor("psum", [P, 8, 512], F32))

        def bank(b, n=1):
            return psum[:, b:b + n, :].rearrange("p a n -> p (a n)")
        ld_vec = sem("ld_vec"); ld_x = sem("ld_x"); ld_con = sem("ld_con"); ones_set = sem("ones_set"); cond_set = sem("cond_set")
        mod_set = sem("mod_set"); row_copied = sem("row_copied"); ada_tp = sem("ada_tp"); blk_done = sem("blk_done")
        squares = sem("squares"); sums = sem("sums"); sums_read = sem("sums_read"); inverse = sem("inverse"); root = sem("root")
        scaled = sem("scaled"); h_ready = sem("h_ready"); lin_act = sem("lin_act"); lin_dve = sem("lin_dve"); spread = sem("spread")
        znorm = sem("znorm"); rot_done = sem("rot_done"); rot_read = sem("rot_read"); qk_ready = sem("qk_ready"); sc_done = sem("sc_done")
        sc_read = sem("sc_read"); mx_ready = sem("mx_ready"); ex_done = sem("ex_done"); p_ready = sem("p_ready"); tp_done = sem("tp_done")
        tp_read = sem("tp_read"); pv_done = sem("pv_done"); attn_ready = sem("attn_ready"); conv_step = sem("conv_step")
        centred = sem("centred"); yscaled = sem("yscaled"); y_ready = sem("y_ready"); sk_done = sem("sk_done"); sk_read = sem("sk_read")
        shifted = sem("shifted"); exped = sem("exped"); picked = sem("picked"); found = sem("found"); looked = sem("looked")
        ranked = sem("ranked"); folded = sem("folded"); number_step = sem("number_step"); valued = sem("valued"); h2_tp = sem("h2_tp")
        h2_tok = sem("h2_tok"); dve_step = sem("dve_step"); topk_step = sem("topk_step"); paced = sem("paced")
        paced_pool = sem("paced_pool"); by_slot = sem("by_slot"); slot_set = sem("slot_set"); halves_set = sem("halves_set")
        hot_a_set = sem("hot_a_set"); hot_b_set = sem("hot_b_set"); hot_c_set = sem("hot_c_set"); away_set = sem("away_set")
        g_made = sem("g_made"); g_laid = sem("g_laid"); hsplit = sem("hsplit"); uhi_set = sem("uhi_set"); ulo_set = sem("ulo_set")
        vhi_set = sem("vhi_set"); vlo_set = sem("vlo_set"); act_done = sem("act_done"); gel_set = sem("gel_set"); w_set = sem("w_set")
        whi_set = sem("whi_set"); wlo_set = sem("wlo_set"); out_done = sem("out_done"); row_used = sem("row_used")
        ix_copied = sem("ix_copied"); dots = sem("dots"); gelued = sem("gelued"); coef = sem("coef"); acc_set = sem("acc_set")
        summed = sem("summed"); evacuated = sem("evacuated"); fin_tp = sem("fin_tp"); fin_read = sem("fin_read"); stored = sem("stored")
        kv_stored = sem("kv_stored")
        ring_in = [sem(f"ring_in{i}") for i in range(RING)]
        u_in, v_in, g_in, g_out = ([sem(f"{n}{i}") for i in range(2)] for n in ("u_in", "v_in", "g_in", "g_out"))
        row_in = [sem(f"row_in{i}") for i in range(GR)]

        block = ctx.enter_context(nc.Block())

        def V(col, n=1):
            return vec[:, col:col + n]

        ident = con[:, C_ID:C_ID + P]
        lin, stat = (bank(0, 2), bank(2, 2)), bank(4, 2)

        def g_group(b):
            per = P // TG
            return ORDER[N_GATHER + b // per] * per + b % per

        def token_of(b):
            return g_group(b * 4 // TG) * TG + b * 4 % TG

        def hot_a_split(b):
            return 1 if b % 4 == 3 else 2

        def final_src(k):
            return accs[k][:, 0, :] if k < N_GATHER else rows[:, k - N_GATHER, 0:D]

        @block.sync
        def _(sp):
            def load(blk, n):
                def one(j, i=None):
                    at = blk + j
                    src = wblk[at] if i is None else wblk[bass.ds(i * RING + at, 1)].rearrange("a p c n -> (a p) c n")
                    sp.wait_ge(blk_done, at - RING + 1 if i is None else i * RING + (at - RING + 1))
                    sp.dma_start(ring[:, at % RING], src).then_inc(ring_in[at % RING], 16)
                whole = n // RING
                with sp.Fori(0, whole) as i:
                    for j in range(RING):
                        one(j, i)
                for j in range(whole * RING, n):
                    one(j)

            sp.dma_start(vec[:], vecs).then_inc(ld_vec, 16)
            for j in range(2):
                sp.dma_start(ring[:, j], wblk[j]).then_inc(ring_in[j], 16)
            sp.dma_start(x[:], x_in).then_inc(ld_x, 16)
            for j in range(2, RING):
                sp.dma_start(ring[:, j], wblk[j]).then_inc(ring_in[j], 16)
            for dst, src in ((con[:], consts), (kc, kctx), (vc, vctx), (keyT, keys)):
                sp.dma_start(dst, src).then_inc(ld_con, 16)
            load(RING, S_END - RING)

            for b in range(NG):
                sp.wait_ge(g_laid, 8 * (b + 1))
                sp.dma_start(g_dram[g_group(b)], gbuf[:, b % 2].rearrange("p k t -> p (k t)")).then_inc(g_out[b % 2], 16)
            tv = table.rearrange("(i j) n -> j i n", j=KEYS)
            gv = g_dram.rearrange("g i (q m) -> q i g m", q=KEYS // QUAD)

            def weights_quad(i, q_):
                sp.dma_start(gin[:, q_], gv[bass.ds(i * (JB // QUAD) + q_, 1)].rearrange("a i g m -> (a i) g m")).then_inc(g_in[q_], 16)

            def expert_step(i, first):
                for jj in range(JB):
                    b = jj % 2
                    if jj % QUAD == 0 and not (first and jj == 0):
                        if not first:
                            sp.wait_ge(w_set, i * JB + (jj - QUAD))
                        weights_quad(i, jj // QUAD)
                    if not (first and jj < 2):
                        sp.wait_ge(ulo_set, i * JB + (jj - 1))
                    sp.dma_start(uraw[:, b], ublk[bass.ds(i * JB + jj, 1)].rearrange("a p c n -> (a p) c n")).then_inc(u_in[b], 16)
                    if not (first and jj < 2):
                        sp.wait_ge(vlo_set, i * JB + (jj - 1))
                    sp.dma_start(vraw[:, b], tv[bass.ds(i * JB + jj, 1), :, D:2 * D].rearrange("a i n -> (a i) n")).then_inc(v_in[b], 16)
                    if first and jj == 1:
                        for h_ in range(2):
                            sp.wait_ge(g_out[h_], 16 * (NG // 2))
                        weights_quad(i, 0)

            sp.wait_ge(g_made, ND // 4)
            sp.wait_ge(hsplit, 2)
            sp.wait_ge(h2_tok, 2 * N_GATHER)
            expert_step(0, True)
            with sp.Fori(1, STEPS) as i:
                expert_step(i, False)
            for k in range(TILES):
                t = ORDER[k]
                sp.wait_ge(fin_read, DC * (k + 1))
                sp.dma_start(y_out[:, :, t * P:(t + 1) * P], x[:, :, t * P:(t + 1) * P]).then_inc(stored, 16)
            sp.wait_ge(stored, 16 * TILES)

        @block.tensor
        def _(pe):
            def weights(seq, i=None):
                n = 16 * (seq // RING + 1)
                pe.wait_ge(ring_in[seq % RING], n if i is None else i * 16 + n)
                return ring[:, seq % RING]

            def ada(seq, b):
                for j in range(ADA_G):
                    w = weights(seq + j)
                    for c in range(DC):
                        last = pe.matmul(psum[0:2, b, j * P:(j + 1) * P], scond[:, c, :], w[:, c, :], start=(c == 0), stop=(c == DC - 1))
                    last.then_inc(blk_done, 1)

            def ada_turn(rows_, b, g):
                for j in range(ADA_G):
                    col = 2 * (ADA_G * g + j)
                    last = pe.transpose(psum[:, b, col:col + 2], rows_[0:2, j * P:(j + 1) * P], con[0:2, C_ID:C_ID + 2])
                return last

            def both(dst, w, src, l0, p0, start, stop):
                pe.matmul(dst[:, 0:512], w, src[:, l0:l0 + T_L], start=start, stop=stop)
                return pe.matmul(dst[:, 512:N], w, src[:, p0:p0 + T_P], start=start, stop=stop)

            def column_sum(src, chunks, k):
                if k:
                    pe.wait_ge(sums_read, k)
                for c in range(chunks):
                    last = both(stat, ones[:], src[:, c, :], 0, T_L, c == 0, c == chunks - 1)
                last.then_inc(sums, 1)

            def linear(dst, w, src, chunks=DC, p0=T_L, fresh=None):
                for c in range(chunks):
                    if fresh is not None:
                        pe.wait_ge(h_ready, fresh + c + 1)
                    last = both(dst, w[:, c, :], src[:, c, :], 0, p0, c == 0, c == chunks - 1)
                last.then_inc(blk_done, 1)

            pe.wait_ge(ones_set, 1)
            pe.wait_ge(cond_set, 1)
            groups1 = N_ADA1 // ADA_G
            for g in range(groups1):
                if g == groups1 // 2:
                    pe.wait_ge(squares, 1)
                    column_sum(h, DC, 0)
                ada(S_ADA1 + ADA_G * g, g)
            pe.wait_ge(ld_con, 64)
            pe.wait_ge(row_copied, groups1)
            for g in range(groups1):
                last = ada_turn(modrow[0][:, g], 7, g)
            last.then_inc(ada_tp, 1)
            for b in range(N_IN):
                if b >= 2:
                    pe.wait_ge(lin_act, b - 1)
                w = weights(S_IN + b)
                if b == IN_V:
                    for t in range(TILES):
                        for c in range(DC):
                            last = pe.matmul(lin[b % 2][:, t * P:(t + 1) * P], h[:, c, t * P:(t + 1) * P], w[:, c, :],
                                             start=(c == 0), stop=(c == DC - 1))
                    last.then_inc(blk_done, 1)
                else:
                    linear(lin[b % 2], w, h, fresh=None if b else 0)
            pe.wait_ge(lin_act, N_IN)
            pe.wait_ge(sums_read, 1)
            for c in range(QK):
                last = both(stat[0:2 * QK], con[:, C_SUM + 10 * c:C_SUM + 10 * c + 10], zsq[:, c, :], 0, T_L, c == 0, c == QK - 1)
            last.then_inc(sums, 1)
            for g in range(ADA_EARLY):
                ada(S_ADA2 + ADA_G * g, g)
            pe.wait_ge(root, 2)
            for c in range(QK):
                pe.wait_ge(sums_read, 2) if c < 1 else pe.wait_ge(znorm, c)
                both(stat, con[0:2 * QK, C_SPREAD + P * c:C_SPREAD + P * (c + 1)], rq[0:2 * QK, :], 0, T_L, True, True).then_inc(spread, 1)
            pe.wait_ge(mod_set, 1)
            for c in range(QK):
                pe.wait_ge(znorm, c + 1)
                if c >= 2:
                    pe.wait_ge(rot_read, c - 1)
                pe.matmul(psum[:, 6 + c % 2, :], con[:, C_ROT:C_ROT + P], z[:, c, 0:T_L], start=True, stop=True).then_inc(rot_done, 1)

            def score(un):
                t, g, spans, _, _ = UNITS[un]
                part = slice(HD * g, HD * g + HD)
                for c in range(QC):
                    k = 4 * un + c
                    if k >= 2:
                        pe.wait_ge(sc_read, k - 1)
                    for at, own, t0, m in spans:
                        kt = z[part, 0, t0 * P:(t0 + m) * P] if own else kc[part, :]
                        last = pe.matmul(psum[:, 6 + c % 2, at * P:(at + m) * P], z[part, 1 + c, t * P:(t + 1) * P], kt, start=True, stop=True)
                    last.then_inc(sc_done, 1)

            def values(un):
                t, g, spans, _, nk = UNITS[un]
                for c in range(QC):
                    k = 4 * un + c
                    pe.wait_ge(p_ready, k + 1)
                    if k >= 2:
                        pe.wait_ge(tp_read, k - 1)
                    for b in range(nk):
                        last = pe.transpose(psum[:, 2 * (k % 2), b * P:(b + 1) * P], sm[:, un % 2, c, b * P:(b + 1) * P], ident)
                    last.then_inc(tp_done, 1)
                pe.wait_ge(tp_read, 4 * un + 4)
                if un >= 2:
                    pe.wait_ge(attn_ready, un - 1)
                kb = 0
                for at, own, t0, m in spans:
                    for j in range(m):
                        v = vtok[:, t0 + j, HD * g:HD * g + HD] if own else vc[:, HD * g:HD * g + HD]
                        last = pe.matmul(psum[HD * g:HD * g + HD, 1 + 2 * (un % 2), :], v, pt[:, un % 2, at + j].rearrange("p h n -> p (h n)"),
                                         start=(kb == 0), stop=(kb == nk - 1))
                        kb += 1
                last.then_inc(pv_done, 1)

            def conv_sum(src):
                for c in range(CC):
                    pe.matmul(psum[:, 4, :], ones[:], src[:, c, 0:512], start=(c == 0), stop=(c == CC - 1))
                    last = pe.matmul(psum[:, 5, 0:NY - 512], ones[:], src[:, c, 512:NY], start=(c == 0), stop=(c == CC - 1))
                last.then_inc(sums, 1)

            pe.wait_ge(znorm, QK)
            pe.wait_ge(conv_step, CC * TAPS)
            conv_sum(y)
            pe.wait_ge(rot_read, QK)
            score(0)
            pe.wait_ge(sums_read, 3)
            pe.wait_ge(squares, 2)
            conv_sum(view(0, CC, NY))
            pe.wait_ge(sums_read, 4)
            pe.wait_ge(row_copied, groups1 + ADA_EARLY)
            for g in range(ADA_EARLY):
                ada_turn(modrow[1][:, g], 5, g)
            late = N_ADA2 // ADA_G - ADA_EARLY
            for un in range(len(UNITS)):
                if un + 1 < len(UNITS):
                    if un + 1 == 2:
                        pe.wait_ge(qk_ready, QK)
                    score(un + 1)
                if 2 <= un < late + 2:
                    g = ADA_EARLY + un - 2
                    pe.wait_ge(row_copied, groups1 + g + 1)
                    last = ada_turn(modrow[1][:, g % 4], 5, g)
                    if un == late + 1:
                        last.then_inc(ada_tp, 1)
                if 1 <= un <= late:
                    ada(S_ADA2 + ADA_G * (ADA_EARLY + un - 1), 4)
                values(un)
            pe.wait_ge(y_ready, CC)
            pe.wait_ge(attn_ready, len(UNITS))
            for b in range(N_PW):
                if b >= 2:
                    pe.wait_ge(lin_act, N_IN + b - 1)
                linear(lin[b % 2], weights(S_PW + b), y, CC, YP)
            pe.wait_ge(lin_act, N_IN + N_PW)

            def out_blocks(i, first):
                for j in range(RING):
                    pe.wait_ge(lin_dve, max(j - 1, 0) + 1 if first else i * RING + j)
                    linear(lin[j % 2], weights(S_OUT + j, None if first else i), mix)
                    if not first or j >= 2:
                        pe.wait_ge(squares, 2 + j - 1 if first else i * RING + (2 + j - 1))
                        src = h[:, j - 2, :] if first else h[:, bass.ds(i * RING + (j - 2), 1), :].rearrange("p a n -> p (a n)")
                        both(stat, ones[:], src, 0, T_L, first and j == 2, False)

            pe.wait_ge(mod_set, 2)
            out_blocks(0, True)
            with pe.Fori(1, N_OUT // RING) as i:
                out_blocks(i, False)
            for c in range(DC - 2, DC):
                pe.wait_ge(squares, 2 + c + 1)
                last = both(stat, ones[:], h[:, c, :], 0, T_L, False, c == DC - 1)
            last.then_inc(sums, 1)
            pe.wait_ge(lin_dve, N_OUT + 1)

            def key_scores(b, i=None):
                at = b % RING
                pe.wait_ge(lin_act, N_IN + N_PW + b + 1 if i is None else i * RING + (N_IN + N_PW + b + 1))
                if i is None:
                    if b >= 2:
                        pe.wait_ge(sk_read, b - 1)
                else:
                    pe.wait_ge(sk_read, i * RING + (b - 1))
                kt = keyT[:, b, :] if i is None else keyT[:, bass.ds(i * RING + b, 1), :].rearrange("p a n -> p (a n)")
                for k, t in enumerate(ORDER):
                    b0 = 4 + 2 * (b % 2) + k // 4
                    last = pe.matmul(psum[:, b0, (k % 4) * P:(k % 4 + 1) * P], q[:, at, t * P:(t + 1) * P], kt, start=True, stop=True)
                last.then_inc(sk_done, 1)

            def query_blocks(i, first):
                for j in range(RING):
                    pe.wait_ge(lin_act, N_IN + N_PW + max(j - 1, 0) if first else i * RING + (N_IN + N_PW + j - 1))
                    linear(lin[j % 2], weights(S_WQ + j, None if first else i), h, fresh=DC if first and j == 0 else None)
                    if not first or j:
                        key_scores(j - 1, None if first else i)

            query_blocks(0, True)
            with pe.Fori(1, N_WQ // RING) as i:
                query_blocks(i, False)
            key_scores(SB - 1)
            for k in range(N_GATHER):
                t = ORDER[k]
                for half in range(2):
                    for c in range(4):
                        last = pe.transpose(psum[:, 2 * k + half, c * P:(c + 1) * P], h[:, 4 * half + c, t * P:(t + 1) * P], ident)
                    last.then_inc(h2_tp, 1)
            pe.wait_ge(sk_read, SB)
            for g in range(N_ADA3 // ADA_G):
                ada(S_ADA3 + ADA_G * g, 4 + g)
            pe.wait_ge(row_copied, groups1 + (N_ADA2 + N_ADA3) // ADA_G)
            for g in range(N_ADA3 // ADA_G):
                last = ada_turn(modrow[2][:, g], 6, g)
            last.then_inc(ada_tp, 1)
            pe.wait_ge(h2_tok, 2 * N_GATHER)
            for k in range(N_DENSE):
                pe.wait_ge(picked, 1)
                pe.transpose(psum[:, k, 0:P], ef[:, N_GATHER + k, :], ident)
                pe.transpose(psum[:, k, P:2 * P], gw[:, N_GATHER + k, :], ident).then_inc(by_slot, 1)
            pe.wait_ge(mod_set, 3)
            for b in range(ND // 4):
                pe.wait_ge(hot_a_set, b + 1)
                pe.wait_ge(hot_b_set, b + 1)
                pe.wait_ge(hot_c_set, b + 1)
                if b >= 4:
                    pe.wait_ge(g_laid, b - 3)
                for m in range(4):
                    last = pe.matmul(psum[:, 4 + b % 4, m * P:(m + 1) * P], hot_a[:, b % 4, m, :], hot_b[:, b % 4, m, :], start=True, stop=True)
                last.then_inc(g_made, 1)
            pe.wait_ge(g_laid, ND // 4)
            pe.wait_ge(hsplit, 2)

            def activations(i, jj, first):
                b = jj % 2
                pe.wait_ge(uhi_set, i * JB + (jj + 1))
                pe.wait_ge(ulo_set, i * JB + (jj + 1))
                if not (first and jj < 2):
                    pe.wait_ge(gel_set, i * JB + (jj - 1))
                n = 0
                for c in range(DC):
                    for w, m in ((uhi, hhi), (uhi, hlo), (ulo, hhi)):
                        last = pe.matmul(psum[:, b, 0:ND], w[:, b, c, :], m[:, c, :], start=(n == 0), stop=(n == 3 * DC - 1))
                        n += 1
                last.then_inc(act_done, 1)

            def outputs(i, jj, start, stop):
                b = jj % 2
                for s_ in (whi_set, wlo_set, vhi_set, vlo_set):
                    pe.wait_ge(s_, i * JB + (jj - 1))
                for t in range(N_DENSE):
                    for half in range(2):
                        for k, (w, m) in enumerate(((whi, vhi), (whi, vlo), (wlo, vhi))):
                            last = pe.matmul(psum[:, 2 + 2 * t + half, :], w[:, b, t * P:(t + 1) * P], m[:, b, 512 * half:512 * (half + 1)],
                                             start=start and k == 0, stop=stop and k == 2)
                last.then_inc(out_done, 1)

            for jj in range(JB):
                activations(0, jj, True)
                if jj >= 2:
                    outputs(0, jj, jj == 2, False)
            with pe.Fori(1, STEPS) as i:
                for jj in range(JB):
                    activations(i, jj, False)
                    outputs(i, jj, False, False)
            outputs(STEPS, 0, False, False)
            outputs(STEPS, 1, False, True)
            for k in range(TILES):
                if k < N_GATHER:
                    pe.wait_ge(summed, k + 1)
                else:
                    pe.wait_ge(evacuated, k - N_GATHER + 1)
                for half in range(2):
                    if k:
                        pe.wait_ge(fin_read, DC * (k - 1) + 4 * half + 4)
                    for c in range(4):
                        last = pe.transpose(psum[:, half, c * P:(c + 1) * P], final_src(k)[:, (4 * half + c) * P:(4 * half + c + 1) * P], ident)
                    last.then_inc(fin_tp, 1)

        @block.scalar
        def _(act):
            def add_shift(half, col):
                for c in range(DC):
                    act.wait_ge(scaled, DC * half + c + 1)
                    act.activation(h[:, c, 0:T_L], h[:, c, 0:T_L], ACT.Identity, bias=mod[:, col + c, 0:1])
                    act.activation(h[:, c, T_L:N], h[:, c, T_L:N], ACT.Identity, bias=mod[:, col + c, 1:2]).then_inc(h_ready, 1)

            act.wait_ge(ld_vec, 16)
            act.activation(scond[:].rearrange("p c k -> p (c k)"), V(V_COND, 2 * DC), ACT.Silu).then_inc(cond_set, 1)
            act.wait_ge(ld_x, 16)
            act.activation(h, x[:], ACT.Square).then_inc(squares, 1)

            def copy_rows(seq, dst, b):
                act.wait_ge(blk_done, seq + ADA_G)
                act.copy(dst[0:2, :], psum[0:2, b, :]).then_inc(row_copied, 1)

            groups1 = N_ADA1 // ADA_G
            for g in range(groups1):
                if g == groups1 // 2:
                    act.wait_ge(inverse, 1)
                    act.activation(rb[:, 0:N], rb[:, 0:N], ACT.Sqrt).then_inc(root, 1)
                copy_rows(S_ADA1 + ADA_G * g, modrow[0][:, g], g)
            add_shift(0, M_SH1)
            for b in range(N_IN):
                act.wait_ge(blk_done, S_IN + b + 1)
                src = lin[b % 2][:, 0:N]
                if b == IN_V:
                    act.copy(vtok.rearrange("p t n -> p (t n)"), src).then_inc(lin_act, 1)
                elif b >= IN_K:
                    c = max(b - IN_V, 0)
                    act.copy(z[:, c, :], src)
                    act.activation(zsq[:, c, :], src, ACT.Square).then_inc(lin_act, 1)
                else:
                    left, right, func = (ga, gap, ACT.Copy) if b % 2 == 0 else (gg, ggp, ACT.Sigmoid)
                    act.activation(left[:, b // 2, :], src[:, 0:T_L], func)
                    act.activation(right[:, b // 2, :], src[:, T_L:N], func).then_inc(lin_act, 1)
            for g in range(ADA_EARLY):
                copy_rows(S_ADA2 + ADA_G * g, modrow[1][:, g], g)
            act.wait_ge(inverse, 2)
            act.activation(rq[0:2 * QK, :], rq[0:2 * QK, :], ACT.Sqrt).then_inc(root, 1)

            def exps(un):
                _, _, _, _, nk = UNITS[un]
                act.wait_ge(mx_ready, un + 1)
                b = un % 2
                for c in range(QC):
                    act.activation(sm[:, b, c, 0:nk * P], sm[:, b, c, 0:nk * P], ACT.Exp, bias=nm[:, b, c:c + 1], accum_out=rs[:, b, c:c + 1])
                act.activation(es[:, b, :], sd[:, b, :], ACT.Exp).then_inc(ex_done, 1)

            act.wait_ge(centred, CC)
            act.activation(view(0, CC, NY), y, ACT.Square).then_inc(squares, 1)
            exps(0)
            act.wait_ge(inverse, 3)
            act.activation(rb, rb, ACT.Sqrt).then_inc(root, 1)
            for c in range(CC):
                act.wait_ge(yscaled, c + 1)
                act.activation(y[:, c, :], y[:, c, :], ACT.Silu, bias=V(V_LB + c), scale=V(V_LG + c)).then_inc(y_ready, 1)
            for un, (t, g, _, _, nk) in enumerate(UNITS):
                group = ADA_EARLY + un - 1
                if ADA_EARLY <= group < N_ADA2 // ADA_G:
                    copy_rows(S_ADA2 + ADA_G * group, modrow[1][:, group % 4], 4)
                if un >= 2:
                    act.wait_ge(pv_done, un - 1)
                for c in range(QC):
                    k = 4 * un + c
                    act.wait_ge(tp_done, k + 1)
                    act.copy(pt[:, un % 2, 0:nk, c, :], psum[:, 2 * (k % 2), 0:nk * P].rearrange("p (k n) -> p k n", k=nk)).then_inc(tp_read, 1)
                if un + 1 < len(UNITS):
                    exps(un + 1)
                act.wait_ge(pv_done, un + 1)
                act.copy(mix[HD * g:HD * g + HD, 0:QC, t * P:(t + 1) * P],
                         psum[HD * g:HD * g + HD, 1 + 2 * (un % 2), :].rearrange("p (h n) -> p h n", h=QC)).then_inc(attn_ready, 1)
            act.dma_start(o_k, z[:, 0, T_L:N]).then_inc(kv_stored, 16)
            act.dma_start(o_v, vtok[:, TP, :]).then_inc(kv_stored, 16)
            for b in range(N_PW):
                act.wait_ge(blk_done, S_PW + b + 1)
                act.copy(mix[:, QC + b, :], lin[b % 2][:, 0:N]).then_inc(lin_act, 1)
            with act.Fori(0, N_OUT) as i:
                act.wait_ge(lin_dve, i + 2)
                act.activation(h[:, bass.ds(i, 1), :], x[:, bass.ds(i, 1), :], ACT.Square).then_inc(squares, 1)
            act.wait_ge(inverse, 4)
            act.activation(rb[:, 0:N], rb[:, 0:N], ACT.Sqrt).then_inc(root, 1)
            add_shift(1, M_SH2)
            act.wait_ge(kv_stored, 32)

            def queries(i, first):
                for j in range(RING):
                    act.wait_ge(blk_done, S_WQ + j + 1 if first else i * RING + (S_WQ + j + 1))
                    if not first:
                        act.wait_ge(sk_done, i * RING + (j + 1 - RING))
                    act.copy(q[:, j, :], lin[j % 2][:, 0:N]).then_inc(lin_act, 1)

            queries(0, True)
            with act.Fori(1, N_WQ // RING) as i:
                queries(i, False)
            for k in range(N_GATHER):
                for half in range(2):
                    act.wait_ge(h2_tp, 2 * k + half + 1)
                    act.copy(h2tok[:, k, 512 * half:512 * (half + 1)], psum[:, 2 * k + half, :]).then_inc(h2_tok, 1)
            act.copy(hhi[:], h[:, :, 0:ND]).then_inc(hsplit, 1)
            for g in range(N_ADA3 // ADA_G):
                copy_rows(S_ADA3 + ADA_G * g, modrow[2][:, g], 4 + g)
            act.wait_ge(shifted, 1)
            act.activation(ex, ex, ACT.Exp).then_inc(exped, 1)
            for k in range(N_DENSE):
                t = ORDER[N_GATHER + k]
                act.wait_ge(by_slot, k + 1)
                act.copy(eT[:, t * P:(t + 1) * P], psum[:, k, 0:P])
                act.copy(gT[:, t * P:(t + 1) * P], psum[:, k, P:2 * P])
                act.activation(gnT[:, t * P:(t + 1) * P], psum[:, k, P:2 * P], ACT.Copy, scale=-1.0).then_inc(slot_set, 1)

            def distance(b):
                if b % (P // 4) == 0:
                    act.wait_ge(halves_set, b * 4 // P + 1)
                col = token_of(b) + 3
                act.activation(away[:, b % 4, :], con[:, C_IOTA:C_IOTA + KEYS], ACT.Abs, bias=e2T[:, col:col + 1], scale=-1.0).then_inc(away_set, 1)

            def hot_row(b):
                col = token_of(b) + 3
                act.wait_ge(away_set, b + 1)
                if b >= 4:
                    act.wait_ge(g_made, b - 3)
                act.activation(hot_b[:, b % 4, 3, :], away[:, b % 4, :], ACT.Relu, bias=gT[:, col:col + 1], scale=gnT[:, col:col + 1])\
                    .then_inc(hot_c_set, 1)

            act.wait_ge(slot_set, N_DENSE)
            for b in range(3):
                distance(b)
            for b in range(2):
                hot_row(b)
            for b in range(ND // 4):
                if b + 3 < ND // 4:
                    distance(b + 3)
                if b + 2 < ND // 4:
                    hot_row(b + 2)
                group, m = divmod(b, TG // 4)
                act.wait_ge(g_made, b + 1)
                if m == 0 and group >= 2:
                    act.wait_ge(g_out[group % 2], 16 * (group // 2))
                act.copy(gbuf[:, group % 2, :, 4 * m:4 * m + 4].rearrange("p k t -> p t k"),
                         psum[:, 4 + b % 4, :].rearrange("p (t k) -> p t k", t=4)).then_inc(g_laid, 1)
            for b in range(2):
                act.wait_ge(g_out[b], 16 * (NG // 2))

            def u_lead(i, jj, first):
                b = jj % 2
                act.wait_ge(u_in[b], i * (16 * JB // 2) + 16 * (jj // 2 + 1))
                if not (first and jj < 2):
                    act.wait_ge(act_done, i * JB + (jj - 1))
                act.copy(uhi[:, b], uraw[:, b]).then_inc(uhi_set, 1)

            def v_lead(i, jj, first):
                b = 1 - jj % 2
                act.wait_ge(v_in[b], i * (16 * JB // 2) + 16 * ((jj - 1) // 2 + 1))
                if not (first and jj < 3):
                    act.wait_ge(out_done, i * JB + (jj - 2))
                act.copy(vhi[:, b, :], vraw[:, b, :]).then_inc(vhi_set, 1)

            def w_lead(i, jj):
                act.wait_ge(w_set, i * JB + (jj - 1))
                act.copy(whi[:, jj % 2, :], wgt[:, jj % 2, :]).then_inc(whi_set, 1)

            def gelu(i, jj):
                b = 1 - jj % 2
                act.wait_ge(act_done, i * JB + jj)
                act.activation(gel[:, b, :], psum[:, b, 0:ND], ACT.Gelu).then_inc(gel_set, 1)

            def coefficients(i, k, jj):
                c0 = 2 * ((jj - 1) % JB)
                act.wait_ge(dots, i * (GB // 2) + (jj + 1))
                act.activation(ge[:, c0:c0 + 2], av[:, c0:c0 + 2], ACT.Gelu).then_inc(gelued, 1)
                act.wait_ge(gelued, i * (GB // 2) + jj)
                for e in range(2):
                    g_col = bass.ds(i * GB + (2 * jj - 2 + e - k * SLOTS), 1)
                    last = act.activation(cf[:, c0 + e:c0 + e + 1], gw[:, k, g_col], ACT.Copy, scale=ge[:, c0 + e:c0 + e + 1])
                last.then_inc(coef, 1)

            def expert_step(i, k, before, first=False):
                for jj in range(JB):
                    u_lead(i, jj, first)
                    if not (first and jj < 1):
                        v_lead(i, jj, first)
                    if not (first and jj < 2):
                        w_lead(i, jj)
                    if not (first and jj < 1):
                        coefficients(i, k if jj else before, jj)
                        gelu(i, jj)

            expert_step(0, 0, 0, True)
            for k in range(N_GATHER):
                if k:
                    expert_step(k * GSTEPS, k, k - 1)
                with act.Fori(k * GSTEPS + 1, (k + 1) * GSTEPS) as i:
                    expert_step(i, k, k)
            v_lead(STEPS, 0, False)
            w_lead(STEPS, 0)
            coefficients(STEPS, N_GATHER - 1, 0)
            gelu(STEPS, 0)
            w_lead(STEPS, 1)
            for t in range(N_DENSE):
                k = N_GATHER + t
                act.wait_ge(out_done, KEYS)
                act.wait_ge(summed, N_GATHER)
                act.copy(final_src(k), bank(2 + 2 * ORDER[k], 2)).then_inc(evacuated, 1)

        @block.vector
        def _(v):
            steps = [0]

            def step(ins):
                steps[0] += 1
                return ins.then_inc(dve_step, 1)

            def settle():
                v.wait_ge(dve_step, steps[0])

            def read_mod(k, b, n, col):
                v.wait_ge(ada_tp, k)
                bias = V(V_BADA + col, n).unsqueeze(2).broadcast_to([P, n, 2])
                v.tensor_tensor(mod[:, col:col + n, :], psum[:, b, 0:2 * n].rearrange("p (c k) -> p c k", k=2), bias, ALU.add).then_inc(mod_set, 1)
                v.wait_ge(mod_set, k)

            def norm_gain(half, scale_col, norm_col):
                for k in range(2):
                    step(v.scalar_tensor_tensor(out=gain[:, half, k, :], in0=mod[:, scale_col:scale_col + DC, k], scalar=1.0,
                                                in1=V(norm_col, DC), op0=ALU.add, op1=ALU.mult))
                settle()

            def inverse_mean(k, r, src, width):
                v.wait_ge(sums, k)
                v.tensor_scalar(r, src, 1.0 / width, EPS, ALU.mult, ALU.add).then_inc(sums_read, 1)
                v.wait_ge(sums_read, k)
                v.reciprocal(r, r).then_inc(inverse, 1)

            def rms_scale(half, root_k):
                v.wait_ge(root, root_k)
                for c in range(DC):
                    v.scalar_tensor_tensor(out=h[:, c, 0:T_L], in0=x[:, c, 0:T_L], scalar=gain[:, half, 0, c:c + 1], in1=rb[:, 0:T_L],
                                           op0=ALU.mult, op1=ALU.mult)
                    v.scalar_tensor_tensor(out=h[:, c, T_L:N], in0=x[:, c, T_L:N], scalar=gain[:, half, 1, c:c + 1], in1=rb[:, T_L:N],
                                           op0=ALU.mult, op1=ALU.mult).then_inc(scaled, 1)

            def taps(k0, k1, pair):
                for k in range(k0, k1):
                    for e in range(2):
                        c = 2 * pair + e
                        src = gl[:, c, k:k + NY]
                        w = V(V_CW + TAPS * c + k)
                        if k == 0:
                            ins = v.tensor_scalar(y[:, c, :], src, w, V(V_CB + c), ALU.mult, ALU.add)
                        else:
                            v.wait_ge(conv_step, 2 * TAPS * pair + 2 * k + e - 1)
                            ins = v.scalar_tensor_tensor(out=y[:, c, :], in0=src, scalar=w, in1=y[:, c, :], op0=ALU.mult, op1=ALU.add)
                        ins.then_inc(conv_step, 1)

            for counter in (lin_dve, dots, row_used):
                v.sem_inc(counter, 1)
            v.wait_ge(ld_vec, 16)
            v.wait_ge(ld_x, 16)
            inverse_mean(1, rb[:, 0:N], stat[:, 0:N], D)
            read_mod(1, 7, N_ADA1, M_SH1)
            norm_gain(0, M_SC1, V_NORM1)
            rms_scale(0, 1)
            step(v.memset(gl[:, :, 0:PAD], 0.0))
            step(v.memset(gl[:, :, PAD + T_L:2 * PAD + T_L], 0.0))
            step(v.memset(gl[:, :, GLW - PAD:], 0.0))
            for pair in range(CC // 2):
                two = slice(2 * pair, 2 * pair + 2)
                v.wait_ge(lin_act, 4 * (pair + 1))
                step(v.tensor_tensor(gl[:, two, PAD:PAD + T_L], ga[:, two], gg[:, two], ALU.mult))
                step(v.tensor_tensor(gl[:, two, 2 * PAD + T_L:GLW - PAD], gap[:, two], ggp[:, two], ALU.mult))
                settle()
                taps(0, TAPS, pair)
            inverse_mean(2, rq[0:2 * QK, :], stat[0:2 * QK, 0:N], HD)
            for c in range(QK):
                v.wait_ge(spread, c + 1)
                v.scalar_tensor_tensor(out=z[:, c, :], in0=z[:, c, :], scalar=V(V_QG if c else V_KG), in1=stat[:, 0:N],
                                       op0=ALU.mult, op1=ALU.mult).then_inc(znorm, 1)
            for c in range(QK):
                v.wait_ge(znorm, c + 1)
                if c >= 2:
                    v.wait_ge(qk_ready, c - 1)
                step(v.tensor_tensor(rope[:, c % 2, 0, :], z[:, c, 0:T_L], con[:, C_COS:C_COS + T_L], ALU.mult))
                v.wait_ge(rot_done, c + 1)
                v.tensor_tensor(rope[:, c % 2, 1, :], psum[:, 6 + c % 2, :], con[:, C_SIN:C_SIN + T_L], ALU.mult).then_inc(rot_read, 1)
                settle()
                v.wait_ge(rot_read, c + 1)
                v.tensor_tensor(z[:, c, 0:T_L], rope[:, c % 2, 0, :], rope[:, c % 2, 1, :], ALU.add).then_inc(qk_ready, 1)
            def mask_and_max(un):
                t, g, _, m0, nk = UNITS[un]
                w, b = nk * P, un % 2
                if un >= 2:
                    v.wait_ge(tp_done, 4 * (un - 1))
                    v.wait_ge(ex_done, un - 1)
                for c in range(QC):
                    v.wait_ge(sc_done, 4 * un + c + 1)
                    v.scalar_tensor_tensor(out=sm[:, b, c, 0:w], in0=psum[:, 6 + c % 2, 0:w], scalar=SCALE,
                                           in1=con[:, C_MASK + m0 * P:C_MASK + m0 * P + w], op0=ALU.mult, op1=ALU.add).then_inc(sc_read, 1)
                v.wait_ge(sc_read, 4 * un + 4)
                step(v.tensor_reduce(mx[:, b, :], sm[:, b, :, 0:w], AX_X, ALU.max))
                settle()
                sink = V(V_SINK + 4 * g, 4)
                step(v.tensor_tensor(mx[:, b, :], mx[:, b, :], sink, ALU.max))
                settle()
                step(v.tensor_scalar(nm[:, b, :], mx[:, b, :], -1.0, None, ALU.mult))
                v.tensor_tensor(sd[:, b, :], sink, mx[:, b, :], ALU.subtract).then_inc(mx_ready, 1)

            def divide(un):
                b, nk = un % 2, UNITS[un][4]
                v.wait_ge(ex_done, un + 1)
                step(v.tensor_tensor(rd[:, b, :], rs[:, b, :], es[:, b, :], ALU.add))
                settle()
                step(v.reciprocal(rd[:, b, :], rd[:, b, :]))
                settle()
                for c in range(QC):
                    v.tensor_scalar(sm[:, b, c, 0:nk * P], sm[:, b, c, 0:nk * P], rd[:, b, c:c + 1], None, ALU.mult).then_inc(p_ready, 1)

            v.wait_ge(sums, 3)
            v.tensor_scalar(rb, stat[:, 0:NY], 1.0 / (CC * P), None, ALU.mult).then_inc(sums_read, 1)
            v.wait_ge(sums_read, 3)
            v.wait_ge(conv_step, CC * TAPS)
            for c in range(CC):
                v.tensor_tensor(y[:, c, :], y[:, c, :], rb, ALU.subtract).then_inc(centred, 1)
            v.wait_ge(qk_ready, QK)
            mask_and_max(0)
            inverse_mean(4, rb, stat[:, 0:NY], CC * P)
            v.wait_ge(root, 3)
            v.wait_ge(centred, CC)
            for c in range(CC):
                v.tensor_tensor(y[:, c, :], y[:, c, :], rb, ALU.mult).then_inc(yscaled, 1)
            for un in range(len(UNITS)):
                divide(un)
                if un + 1 < len(UNITS):
                    mask_and_max(un + 1)
            read_mod(2, 5, N_ADA2, M_G1)
            norm_gain(1, M_SC2, V_NORM2)
            with v.Fori(0, N_OUT // RING) as i:
                for j in range(RING):
                    v.wait_ge(blk_done, i * RING + (S_OUT + j + 1))
                    for k, (c0, c1) in enumerate(((0, T_L), (T_L, N))):
                        xc = x[:, bass.ds(i * RING + j, 1), c0:c1].rearrange("p a n -> p (a n)")
                        g1 = mod[:, bass.ds(i * RING + (M_G1 + j), 1), k:k + 1].rearrange("p a n -> p (a n)")
                        last = v.scalar_tensor_tensor(out=xc, in0=lin[j % 2][:, c0:c1], scalar=g1, in1=xc, op0=ALU.mult, op1=ALU.add)
                    last.then_inc(lin_dve, 1)
            v.wait_ge(lin_dve, N_OUT + 1)
            inverse_mean(5, rb[:, 0:N], stat[:, 0:N], D)
            rms_scale(1, 4)

            def hold():
                v.sem_inc(paced, 1)

            def numbers(i):
                for t in range(TILES):
                    v.wait_ge(folded, i * TILES + (t + 1 - TILES))
                    v.tensor_reduce(ef[:, t, bass.ds((i - 1) * TOP, TOP)], hit[:, t, :, 0:CAND // 2], AX_X, ALU.add).then_inc(looked, 1)

            def search(i, first):
                k = [0]

                def tk(ins):
                    k[0] += 1
                    return ins.then_inc(topk_step, 1)

                def own():
                    v.wait_ge(topk_step, i * HEAD_STEPS + (1 + k[0]))
                    hold()

                for s_ in range(2):
                    def sc(t):
                        return psum[:, 4 + 2 * s_ + t // 4, (t % 4) * P:(t % 4 + 1) * P]

                    v.wait_ge(sk_done, i * 2 + (s_ + 1))
                    if s_ == 0 and not first:
                        v.wait_ge(number_step, i * NUMBER_STEPS)
                    hold()
                    for t in range(TILES):
                        tk(v.max(best[:, t, s_, 0:8], sc(t)))
                    own()
                    for t in range(TILES):
                        tk(v.max_index(besti[:, t, s_, 0:8], best[:, t, s_, 0:8], sc(t)))
                        tk(v.match_replace(scr[:, s_, t, :], best[:, t, s_, 0:8], sc(t), -3e38))
                    own()
                    v.sem_inc(sk_read, 1)
                    for t in range(TILES):
                        tk(v.max(best[:, t, s_, 8:16], scr[:, s_, t, :]))
                    own()
                    for t in range(TILES):
                        tk(v.max_index(besti[:, t, s_, 8:16], best[:, t, s_, 8:16], scr[:, s_, t, :]))
                own()
                v.sem_inc(ranked, 1)
                if not first:
                    numbers(i)
                at = 0
                for i0, rows_, w in RUNS:
                    shape = [P, TILES, rows_, w]
                    tk(v.tensor_tensor(cand[:, :, at:at + rows_ * w].rearrange("p h (r w) -> p h r w", r=rows_),
                                       best[:, :, 0, i0:i0 + rows_].unsqueeze(3).broadcast_to(shape),
                                       best[:, :, 1, 0:w].unsqueeze(2).broadcast_to(shape), ALU.add))
                    at += rows_ * w
                own()
                for t in range(TILES):
                    tk(v.max(top[:, t, 0:8], cand[:, t, :]))
                own()
                for t in range(TILES):
                    tk(v.max_index(topi[:, t, 0:8], top[:, t, 0:8], cand[:, t, :]))
                    tk(v.match_replace(cand2[:, t, :], top[:, t, 0:8], cand[:, t, :], -3e38))
                own()
                for t in range(TILES):
                    tk(v.max(top[:, t, 8:16], cand2[:, t, :]))
                own()
                for t in range(TILES):
                    tk(v.max_index(topi[:, t, 8:16], top[:, t, 8:16], cand2[:, t, :]))
                tk(v.tensor_tensor(ex[:, :, bass.ds(i, 1), :].rearrange("p t a k -> p t (a k)"), top[:],
                                   top[:, :, 0:1].broadcast_to([P, TILES, TOP]), ALU.subtract))
                own()
                if not first:
                    v.wait_ge(valued, i * TILES)
                    v.wait_ge(looked, i * TILES)
                tk(v.tensor_copy(topf[:], topi[:]))
                own()
                for t in range(TILES):
                    v.tensor_tensor(place[:, t], count[:].unsqueeze(1).broadcast_to([P, TOP, CAND]),
                                    topf[:, t, :].unsqueeze(2).broadcast_to([P, TOP, CAND]), ALU.is_equal).then_inc(found, 1)
                assert k[0] == HEAD_STEPS

            v.tensor_copy(count[:], con[:, C_IOTA:C_IOTA + CAND]).then_inc(topk_step, 1)
            search(0, True)
            with v.Fori(1, PH) as i:
                search(i, False)
            v.wait_ge(topk_step, PH * HEAD_STEPS + 1)
            v.sem_inc(shifted, 1)
            v.wait_ge(hsplit, 1)
            v.tensor_tensor(hlo[:], h[:, :, 0:ND], hhi[:].bitcast(F32), ALU.subtract).then_inc(hsplit, 1)
            numbers(PH)
            v.wait_ge(exped, 1)
            exh = ex.rearrange("p t h k -> p (t h) k")
            step(v.tensor_reduce(den[:], exh, AX_X, ALU.add))
            v.wait_ge(looked, TILES * PH)
            step(v.tensor_copy(idxu[:], ef[:]))
            settle()
            step(v.reciprocal(den[:], den[:]))
            settle()
            v.tensor_tensor(gw[:].rearrange("p t (h k) -> p (t h) k", h=PH), exh, den[:].unsqueeze(2).broadcast_to([P, TILES * PH, TOP]), ALU.mult)\
                .then_inc(picked, 1)

            read_mod(3, 6, N_ADA3, M_G2)
            for k in range(N_DENSE):
                t = ORDER[N_GATHER + k]
                part = slice(t * P, (t + 1) * P)
                v.wait_ge(slot_set, k + 1)
                step(v.tensor_scalar(e1u[:, part], eT[:, part], 7, None, ALU.logical_shift_right))
                step(v.tensor_scalar(e2u[:, part], eT[:, part], KEYS - 1, None, ALU.bitwise_and))
                settle()
                step(v.tensor_copy(e1T[:, part], e1u[:, part]))
                step(v.tensor_copy(e2T[:, part], e2u[:, part]))
                settle()
                v.sem_inc(halves_set, 1)
                for b in range(k * P // 4, (k + 1) * P // 4):
                    if b >= 4:
                        v.wait_ge(g_made, b - 3)
                    for m in range(3):
                        col = token_of(b) + m
                        v.tensor_scalar(hot_b[:, b % 4, m, :], con[:, C_IOTA:C_IOTA + KEYS], e2T[:, col:col + 1], gT[:, col:col + 1],
                                        ALU.is_equal, ALU.mult)
                    m0 = hot_a_split(b)
                    col, wide = token_of(b) + m0, [P, 4 - m0, KEYS]
                    v.tensor_tensor(hot_a[:, b % 4, m0:4, :], con[:, C_IOTA:C_IOTA + KEYS].unsqueeze(1).broadcast_to(wide),
                                    e1T[:, col:col + 4 - m0].unsqueeze(2).broadcast_to(wide), ALU.is_equal).then_inc(hot_b_set, 1)
            for b in range(2):
                v.wait_ge(g_out[b], 16 * (NG // 2))
            v.wait_ge(acc_set, N_GATHER)
            v.wait_ge(h2_tok, 2 * N_GATHER)

            def v_rest(i, jj):
                b = 1 - jj % 2
                v.wait_ge(vhi_set, i * JB + jj)
                v.tensor_tensor(vlo[:, b, :], vraw[:, b, :], vhi[:, b, :].bitcast(F32), ALU.subtract).then_inc(vlo_set, 1)

            def w_rest(i, jj):
                b = jj % 2
                v.wait_ge(whi_set, i * JB + (jj - 1))
                v.wait_ge(w_set, i * JB + (jj - 1))
                v.tensor_tensor(wlo[:, b, :], wgt[:, b, :], whi[:, b, :].bitcast(F32), ALU.subtract).then_inc(wlo_set, 1)

            def weigh(i, jj):
                b = 1 - jj % 2
                v.wait_ge(gel_set, i * JB + jj)
                quad, m = divmod(jj - 1, QUAD)
                v.wait_ge(g_in[quad % 2], i * 16 + (0 if quad < 0 else 16))
                v.tensor_tensor(wgt[:, b, :].rearrange("p (g t) -> p g t", t=TG), gel[:, b, :].rearrange("p (g t) -> p g t", t=TG),
                                gin[:, quad % 2, :, m * TG:(m + 1) * TG], ALU.mult).then_inc(w_set, 1)

            def dot(i, k, jj):
                v.wait_ge(dots, i * (GB // 2) + (jj + 1))
                for e in range(2):
                    sl = 2 * jj + e
                    v.wait_ge(row_in[sl % GR], i * (16 * GB // GR) + 16 * (sl // GR + 1))
                    ins = v.scalar_tensor_tensor(out=junk[:, e, :], in0=rows[:, sl % GR, 0:D], scalar=1.0, in1=h2tok[:, k, :],
                                                 op0=ALU.mult, op1=ALU.mult, accum_out=av[:, sl:sl + 1])
                ins.then_inc(dots, 1)

            def add_rows(i, k, jj):
                v.wait_ge(coef, i * (GB // 2) + jj)
                v.wait_ge(row_used, i * GB + (2 * jj - 1))
                for e in range(2):
                    sl = 2 * ((jj - 1) % JB) + e
                    v.scalar_tensor_tensor(out=accs[k][:, e, :], in0=rows[:, sl % GR, D:2 * D], scalar=cf[:, sl:sl + 1], in1=accs[k][:, e, :],
                                           op0=ALU.mult, op1=ALU.add).then_inc(row_used, 1)

            def expert_step(i, k, before, first=False):
                for jj in range(JB):
                    if not (first and jj < 1):
                        v_rest(i, jj)
                    if not (first and jj < 2):
                        w_rest(i, jj)
                    if not (first and jj < 1):
                        add_rows(i, k if jj else before, jj)
                        weigh(i, jj)
                    dot(i, k, jj)

            expert_step(0, 0, 0, True)
            for k in range(N_GATHER):
                if k:
                    expert_step(k * GSTEPS, k, k - 1)
                with v.Fori(k * GSTEPS + 1, (k + 1) * GSTEPS) as i:
                    expert_step(i, k, k)
            v_rest(STEPS, 0)
            w_rest(STEPS, 0)
            add_rows(STEPS, N_GATHER - 1, 0)
            weigh(STEPS, 0)
            w_rest(STEPS, 1)
            v.wait_ge(row_used, N_GATHER * SLOTS + 1)
            for k in range(N_GATHER):
                v.tensor_tensor(accs[k][:, 0, :], accs[k][:, 0, :], accs[k][:, 1, :], ALU.add).then_inc(summed, 1)
            for k in range(TILES):
                t = ORDER[k]
                for c in range(DC):
                    if c % 4 == 0:
                        v.wait_ge(fin_tp, 2 * k + c // 4 + 1)
                    xc = x[:, c, t * P:(t + 1) * P]
                    v.scalar_tensor_tensor(out=xc, in0=psum[:, c // 4, (c % 4) * P:(c % 4 + 1) * P], scalar=mod[:, M_G2 + c, int(t == TP):int(t == TP) + 1],
                                           in1=xc, op0=ALU.mult, op1=ALU.add).then_inc(fin_read, 1)

        @block.gpsimd
        def _(pool):
            pool.memset(ones[:], 1.0).then_inc(ones_set, 1)
            with pool.Fori(0, PH) as i:
                pool.wait_ge(ranked, i + 1)
                pool.sem_inc(paced_pool, 1)
                pool.tensor_copy(bestf[:], besti).then_inc(number_step, 1)
                pool.wait_ge(number_step, i * NUMBER_STEPS + 1)
                pool.sem_inc(paced_pool, 1)
                pool.tensor_scalar(bestf[:, :, 0, :], bestf[:, :, 0, :], float(KEYS), None, ALU.mult).then_inc(number_step, 1)
                pool.wait_ge(number_step, i * NUMBER_STEPS + 2)
                at = 0
                for i0, rows_, w in RUNS:
                    shape = [P, TILES, rows_, w]
                    pool.tensor_tensor(eid[:, :, at:at + rows_ * w].rearrange("p h (r w) -> p h r w", r=rows_),
                                       bestf[:, :, 0, i0:i0 + rows_].unsqueeze(3).broadcast_to(shape),
                                       bestf[:, :, 1, 0:w].unsqueeze(2).broadcast_to(shape), ALU.add).then_inc(number_step, 1)
                    at += rows_ * w
                pool.wait_ge(number_step, (i + 1) * NUMBER_STEPS)
                for t in range(TILES):
                    pool.wait_ge(found, i * TILES + (t + 1))
                    pool.tensor_tensor(hit[:, t], place[:, t], eid[:, t, :].unsqueeze(1).broadcast_to([P, TOP, CAND]), ALU.mult).then_inc(valued, 1)
                    pool.wait_ge(valued, i * TILES + (t + 1))
                    pool.tensor_tensor(hit[:, t, :, 0:CAND // 2], hit[:, t, :, 0:CAND // 2], hit[:, t, :, CAND // 2:CAND], ALU.add).then_inc(folded, 1)
            def fetch_pair(i, k, q_, wait):
                if q_ % 4 == 0:
                    half = q_ // 4
                    pool.tensor_copy(ixr[:, half, :], idxu[:, k, bass.ds(i * GB + (2 * q_ - k * SLOTS), 8)]).then_inc(ix_copied, 1)
                    pool.wait_ge(ix_copied, i * 2 + (half + 1))
                for e in range(2):
                    sl = 2 * q_ + e
                    if wait:
                        pool.wait_ge(row_used, i * GB + (sl + 2 - GR))
                    pool.sem_inc(paced_pool, 1)
                    pool.indirect_dma_start(out=rows[:, sl % GR, :], out_offset=None, in_=table,
                                            in_offset=bass.IndirectOffsetOnAxis(ap=ixr[:, q_ // 4, sl % 8:sl % 8 + 1], axis=0)).then_inc(row_in[sl % GR], 16)

            pool.wait_ge(row_copied, (N_ADA1 + N_ADA2 + N_ADA3) // ADA_G)
            pool.wait_ge(ada_tp, 3)
            pool.wait_ge(hsplit, 2)
            pool.wait_ge(h2_tok, 2 * N_GATHER)
            for k in range(N_GATHER):
                pool.memset(accs[k], 0.0).then_inc(acc_set, 1)
            for k in range(N_DENSE):
                pool.wait_ge(halves_set, k + 1)
                if k == N_DENSE - 1:
                    fetch_pair(0, 0, 0, False)
                    fetch_pair(0, 0, 1, False)
                for b in range(k * P // 4, (k + 1) * P // 4):
                    if b >= 4:
                        pool.wait_ge(g_made, b - 3)
                    col = token_of(b)
                    for m in range(hot_a_split(b)):
                        last = pool.tensor_scalar(hot_a[:, b % 4, m, :], con[:, C_IOTA:C_IOTA + KEYS], e1T[:, col + m:col + m + 1], None, ALU.is_equal)
                    last.then_inc(hot_a_set, 1)
            def expert_step(i, k, first):
                if first:
                    for b in range(2):
                        pool.wait_ge(g_out[b], 16 * (NG // 2))
                for jj in range(JB):
                    b = jj % 2
                    pool.wait_ge(uhi_set, i * JB + (jj + 1))
                    pool.tensor_tensor(ulo[:, b], uraw[:, b], uhi[:, b].bitcast(F32), ALU.subtract).then_inc(ulo_set, 1)
                    if jj + 1 < JB and not (first and jj == 0):
                        fetch_pair(i, k, jj + 1, True)

            expert_step(0, 0, True)
            for k in range(N_GATHER):
                with pool.Fori(max(1, k * GSTEPS), (k + 1) * GSTEPS) as i:
                    fetch_pair(i, k, 0, True)
                    expert_step(i, k, False)
    return nc


def constants():
    import numpy as np

    con = np.zeros((P, C_END), np.float32)
    con[:, C_ID:C_ID + P] = np.eye(P)
    quarter = HD // 4
    turn = np.zeros((P, P), np.float32)
    for m in range(P):
        if m % (2 * quarter) < quarter:
            turn[m + quarter, m] = -1.0
        else:
            turn[m - quarter, m] = 1.0
    con[:, C_ROT:C_ROT + P] = turn
    q, k = np.arange(P)[:, None], np.arange(P)[None, :]
    con[:, C_MASK + P:C_MASK + 2 * P] = np.where(k >= q, 0.0, MASKED)
    con[:, C_MASK + 3 * P:C_MASK + 4 * P] = np.where(k <= q, 0.0, MASKED)
    con[:, C_IOTA:C_IOTA + KEYS] = np.arange(KEYS)
    for c in range(QK):
        for g in range(2):
            con[HD * g:HD * g + HD, C_SUM + 10 * c + 2 * c + g] = 1.0
            con[2 * c + g, C_SPREAD + P * c + HD * g:C_SPREAD + P * c + HD * g + HD] = 1.0
    inv = (np.float32(10000.0) ** (-np.arange(quarter, dtype=np.float32) / np.float32(quarter))).astype(np.float32)
    t = np.arange(T_L)
    place = np.stack([t // 64, t % 64]).astype(np.float32)
    d = np.arange(P) % HD
    ang = place[d // (2 * quarter)] * inv[d % quarter][:, None]
    con[:, C_COS:C_COS + T_L] = np.cos(ang)
    con[:, C_SIN:C_SIN + T_L] = np.sin(ang)
    return con


def kernel(x_prompt, x_sample, cache_k, cache_v, c, c_ctx, norm1, norm2, w_ada, b_ada, w_in, w_out, q_norm, k_norm, attn_sink,
           conv_dw, conv_dw_b, conv_ln_g, conv_ln_b, conv_pw, peer_wq, peer_keys, peer_u, peer_v):
    import concourse.bacc as bacc
    import numpy as np
    from concourse.bass_utils import run_bass_kernel_spmd

    def by_feature(x):
        x = np.asarray(x)
        return np.ascontiguousarray(x.reshape(x.shape[0], -1, P).transpose(2, 1, 0))

    def blocks(w):
        w = np.asarray(w)
        w = w.reshape(w.shape[0] // P, P, w.shape[1] // P, P).transpose(2, 1, 0, 3)
        return np.pad(w, ((0, 0), (0, 0), (0, DC - w.shape[2]), (0, 0)))

    a = {k: np.asarray(v) for k, v in dict(ada=w_ada[0], win=w_in[0], wout=w_out[0], pw=conv_pw[0], wq=peer_wq[0]).items()}
    pairs = np.concatenate([np.r_[h * HD:(h + 1) * HD, (h + 4) * HD:(h + 5) * HD] for h in range(4)])
    qw = HEADS * HD
    kvw = KV * HD
    uw = CC * P
    order = []
    for j in range(CC):
        order += [np.arange(qw + 2 * kvw + j * P, qw + 2 * kvw + (j + 1) * P), np.arange(qw + 2 * kvw + uw + j * P, qw + 2 * kvw + uw + (j + 1) * P)]
    order += [np.arange(qw, qw + 2 * kvw), pairs]
    ada = blocks(a["ada"])
    wblk = np.concatenate([ada[:N_ADA1], blocks(a["win"][:, np.concatenate(order)]), ada[N_ADA1:N_ADA1 + N_ADA2], blocks(a["pw"]),
                           blocks(a["wout"][np.r_[pairs, qw:D]]), blocks(a["wq"]), ada[N_ADA1 + N_ADA2:]])
    vecs = np.zeros((P, V_END), np.float32)

    def put(col, x):
        x = np.asarray(x)
        vecs[:, col:col + x.shape[1]] = x

    put(V_NORM1, np.asarray(norm1[0]).reshape(DC, P).T)
    put(V_NORM2, np.asarray(norm2[0]).reshape(DC, P).T)
    put(V_BADA, np.asarray(b_ada[0]).reshape(48, P).T)
    put(V_COND, np.stack([np.asarray(c[0]).reshape(DC, P).T, np.asarray(c_ctx).reshape(DC, P).T], -1).reshape(P, 2 * DC))
    put(V_QG, np.tile(np.asarray(q_norm[0]), 2)[:, None])
    put(V_KG, np.tile(np.asarray(k_norm[0]), 2)[:, None])
    put(V_CW, np.asarray(conv_dw[0]).reshape(TAPS, CC, P).transpose(2, 1, 0).reshape(P, CC * TAPS))
    put(V_CB, np.asarray(conv_dw_b[0]).reshape(CC, P).T)
    put(V_LG, np.asarray(conv_ln_g[0]).reshape(CC, P).T)
    put(V_LB, np.asarray(conv_ln_b[0]).reshape(CC, P).T)
    put(V_SINK, np.broadcast_to(np.asarray(attn_sink[0])[None], (P, HEADS)))
    ins = {
        "x_in": by_feature(np.concatenate([np.asarray(x_sample[0]), np.asarray(x_prompt[0])])),
        "wblk": np.ascontiguousarray(wblk),
        "vecs": vecs,
        "consts": constants(),
        "kctx": np.ascontiguousarray(np.asarray(cache_k[0, 0]).reshape(P, kvw).T),
        "vctx": np.ascontiguousarray(np.asarray(cache_v[0, 0]).reshape(P, kvw)),
        "keys": np.ascontiguousarray(np.asarray(peer_keys[0]).reshape(SB, P, P).transpose(2, 0, 1)),
        "table": np.concatenate([np.asarray(peer_u[0]), np.asarray(peer_v[0])], axis=1),
        "ublk": np.ascontiguousarray(np.asarray(peer_u[0]).reshape(KEYS, KEYS, DC, P).transpose(1, 3, 2, 0)),
    }
    outs = {"y_out": (P, DC, N), "o_k": (P, P), "o_v": (P, P)}
    nc = bacc.Bacc("TRN2", target_bir_lowering=False, num_devices=1)
    args = [nc.dram_tensor(n, x.shape, F32, kind="ExternalInput").ap() for n, x in ins.items()]
    args += [nc.dram_tensor(n, x, F32, kind="ExternalOutput").ap() for n, x in outs.items()]
    build(nc, *args)
    got = run_bass_kernel_spmd(nc, [ins], core_ids=[0]).results[0]

    def by_token(y):
        return np.ascontiguousarray(y.transpose(2, 1, 0).reshape(1, y.shape[2], D))

    new_k = np.ascontiguousarray(got["o_k"].T).reshape(1, 1, P, KV, HD)
    new_v = np.ascontiguousarray(got["o_v"]).reshape(1, 1, P, KV, HD)
    return by_token(got["y_out"][:, :, T_L:]), by_token(got["y_out"][:, :, :T_L]), new_k, new_v
```
